# Optimizing a Trainium2 kernel written in Bass

```python
import math
import jax, jax.numpy as jnp
from jax import lax
import numpy as np

D_MODEL = 1024
BATCH = 1
SEQ = 256
DEPTH = 2
DEC_BATCH = 1
DEC_SEQ = 512
PAST_LEN = 128

D_MIX = D_MODEL
D_A = D_MIX // 2
S5_GROUP = 16
S5_GROUPS = D_A // S5_GROUP
S5_STATE = 64
DT_MIN = 1e-3
DT_MAX = 1e-1
D_B = D_MIX - D_A
HEAD_DIM = 64
N_HEADS_B = D_B // HEAD_DIM
DILATED_CONFIGS = ((128, 1), (512, 4), (2048, 16))
ATTN_BLOCK = 64
NEG_BIG = -1e30
D_C = D_MIX // 2
FNET_GROUPS = 4
FNET_GROUP_DIM = D_C // FNET_GROUPS
D_D = D_MIX - D_C
CONV_W = 3
D_FF = 2816
EPS = 1e-6
N_AB = (DEPTH + 1) // 2
N_CD = DEPTH // 2

kernel_name = "hybrid_bidir_s5_dilattn_fnet_shortconv_encoder"

def _rms_norm(x, g):
    xf = x.astype(jnp.float32)
    y = xf * lax.rsqrt(jnp.mean(xf * xf, axis=-1, keepdims=True) + EPS)
    return (y * g.astype(jnp.float32)).astype(x.dtype)

def _modulate(x, shift, scale):
    return x * (1.0 + scale[:, None, :]) + shift[:, None, :]

def _dwconv_centred(x, w):
    pad = CONV_W // 2
    T = x.shape[1]
    xp = jnp.pad(x, ((0, 0), (pad, pad), (0, 0)))
    y = xp[:, 0:T] * w[0]
    for j in range(1, CONV_W):
        y = y + xp[:, j:j + T] * w[j]
    return y

def _s5_discretize(lam_re, lam_im, log_dt, b_re, b_im):
    lam_re, lam_im, log_dt, b_re, b_im = (a.astype(jnp.float32) for a in (lam_re, lam_im, log_dt, b_re, b_im))
    dt = jnp.exp(log_dt)[:, None]
    mag = jnp.exp(lam_re * dt)
    a_re = mag * jnp.cos(lam_im * dt)
    a_im = mag * jnp.sin(lam_im * dt)
    den = lam_re * lam_re + lam_im * lam_im
    coef_re = ((a_re - 1.0) * lam_re + a_im * lam_im) / den
    coef_im = (a_im * lam_re - (a_re - 1.0) * lam_im) / den
    bb_re = coef_re[..., None] * b_re - coef_im[..., None] * b_im
    bb_im = coef_re[..., None] * b_im + coef_im[..., None] * b_re
    return a_re, a_im, bb_re, bb_im

def _diag_linear_op(e1, e2):
    a1r, a1i, b1r, b1i = e1
    a2r, a2i, b2r, b2i = e2
    ar = a2r * a1r - a2i * a1i
    ai = a2r * a1i + a2i * a1r
    br = a2r * b1r - a2i * b1i + b2r
    bi = a2r * b1i + a2i * b1r + b2i
    return ar, ai, br, bi

def _s5_mixer(u, lam_re_f, lam_im_f, log_dt_f, lam_re_b, lam_im_b, log_dt_b,
              b_re, b_im, c_re, c_im, d_skip, w_glu, b_glu):
    Bsz, T, _ = u.shape
    ug = u.astype(jnp.float32).reshape(Bsz, T, S5_GROUPS, S5_GROUP)
    fwd = _s5_discretize(lam_re_f, lam_im_f, log_dt_f, b_re, b_im)
    bwd = _s5_discretize(lam_re_b, lam_im_b, log_dt_b, b_re, b_im)
    cr = c_re.astype(jnp.float32)
    ci = c_im.astype(jnp.float32)

    def one_sequence(us):
        y = jnp.zeros(us.shape, jnp.float32)
        for (a_re, a_im, bb_re, bb_im), rev in ((fwd, False), (bwd, True)):
            bu_re = jnp.einsum("tgc,gpc->tgp", us, bb_re)
            bu_im = jnp.einsum("tgc,gpc->tgp", us, bb_im)
            a_re_t = jnp.broadcast_to(a_re, bu_re.shape)
            a_im_t = jnp.broadcast_to(a_im, bu_re.shape)
            _, _, s_re, s_im = lax.associative_scan(
                _diag_linear_op, (a_re_t, a_im_t, bu_re, bu_im), reverse=rev, axis=0)
            y = y + jnp.einsum("tgp,gcp->tgc", s_re, cr) - jnp.einsum("tgp,gcp->tgc", s_im, ci)
        return y

    y = lax.map(one_sequence, ug)
    y = y + ug * d_skip.astype(jnp.float32).reshape(S5_GROUPS, S5_GROUP)
    y = jax.nn.gelu(y.reshape(Bsz, T, D_A))
    y = y * jax.nn.sigmoid(y @ w_glu.astype(jnp.float32) + b_glu.astype(jnp.float32))
    return y.astype(u.dtype)

def _alibi_slopes(n):
    return jnp.power(2.0, -8.0 * jnp.arange(1, n + 1, dtype=jnp.float32) / n)

def _dilated_branch(q, k, v, slopes, window, dilation):
    Bsz, T, H, hd = q.shape
    R = window // (2 * dilation)
    L = T // dilation
    QB = ATTN_BLOCK
    nb = -(-L // QB)
    halo = -(-R // QB)
    Lp = nb * QB
    KW = (2 * halo + 1) * QB

    def to_sub(a):
        return a.reshape(Bsz, L, dilation, H, hd).transpose(0, 2, 1, 3, 4)

    qs, ks, vs = to_sub(q), to_sub(k), to_sub(v)
    qb = jnp.pad(qs, ((0, 0), (0, 0), (0, Lp - L), (0, 0), (0, 0))).reshape(Bsz, dilation, nb, QB, H, hd)
    kv_pad = ((0, 0), (0, 0), (halo * QB, Lp - L + halo * QB), (0, 0), (0, 0))
    kp = jnp.pad(ks, kv_pad).reshape(Bsz, dilation, nb + 2 * halo, QB, H, hd)
    vp = jnp.pad(vs, kv_pad).reshape(Bsz, dilation, nb + 2 * halo, QB, H, hd)
    kb = jnp.concatenate([kp[:, :, j:j + nb] for j in range(2 * halo + 1)], axis=3)
    vb = jnp.concatenate([vp[:, :, j:j + nb] for j in range(2 * halo + 1)], axis=3)

    s = jnp.einsum("bdnqhe,bdnkhe->bdnhqk", qb, kb,
                   preferred_element_type=jnp.float32) * (1.0 / math.sqrt(hd))
    qi = jnp.arange(QB)[:, None]
    rel = (jnp.arange(KW)[None, :] - halo * QB) - qi
    kpos = (jnp.arange(nb) * QB)[:, None, None] + qi[None] + rel[None]
    valid = (jnp.abs(rel) <= R)[None] & (kpos >= 0) & (kpos < L)
    dist = jnp.abs(rel).astype(jnp.float32) * dilation
    alibi = -slopes[:, None, None] * dist[None]
    s = jnp.where(valid[:, None], s + alibi, NEG_BIG)
    m = jnp.max(s, axis=-1, keepdims=True)
    p = jnp.exp(s - m)
    l = jnp.sum(p, axis=-1)
    o = jnp.einsum("bdnhqk,bdnkhe->bdnqhe", p, vb.astype(jnp.float32))
    o = o / jnp.swapaxes(l, -1, -2)[..., None]

    def from_sub(a):
        a = a.reshape((Bsz, dilation, Lp) + a.shape[4:])[:, :, :L]
        a = jnp.moveaxis(a, 1, 2)
        return a.reshape((Bsz, T) + a.shape[3:])

    return (from_sub(o), from_sub(jnp.swapaxes(m[..., 0], -1, -2)), from_sub(jnp.swapaxes(l, -1, -2)))

def _dilated_mixture_attention(q, k, v):
    slopes = _alibi_slopes(N_HEADS_B)
    outs = [_dilated_branch(q, k, v, slopes, w, d) for (w, d) in DILATED_CONFIGS]
    m_all = jnp.stack([o[1] for o in outs])
    m_top = jnp.max(m_all, axis=0)
    wts = jnp.stack([o[2] for o in outs]) * jnp.exp(m_all - m_top)
    o_all = jnp.stack([o[0] for o in outs])
    y = jnp.sum(wts[..., None] * o_all, axis=0) / jnp.sum(wts, axis=0)[..., None]
    return y.astype(q.dtype)

def _mixer_ab(h, w_in, w_out, lam_re_f, lam_im_f, log_dt_f, lam_re_b, lam_im_b, log_dt_b,
              b_re, b_im, c_re, c_im, d_skip, w_glu, b_glu, q_g, k_g):
    Bsz, T, _ = h.shape
    z = h @ w_in
    u, q, k, v = jnp.split(z, [D_A, D_A + D_B, D_A + 2 * D_B], axis=-1)
    y_a = _s5_mixer(u, lam_re_f, lam_im_f, log_dt_f, lam_re_b, lam_im_b, log_dt_b,
                    b_re, b_im, c_re, c_im, d_skip, w_glu, b_glu)
    q = _rms_norm(q.reshape(Bsz, T, N_HEADS_B, HEAD_DIM), q_g)
    k = _rms_norm(k.reshape(Bsz, T, N_HEADS_B, HEAD_DIM), k_g)
    v = v.reshape(Bsz, T, N_HEADS_B, HEAD_DIM)
    y_b = _dilated_mixture_attention(q, k, v).reshape(Bsz, T, D_B)
    return jnp.concatenate([y_a, y_b], axis=-1) @ w_out

def _mixer_cd(h, w_in, w_out, sconv_w):
    Bsz, T, _ = h.shape
    z = h @ w_in
    uc, hs, gb, gc = jnp.split(z, [D_C, D_C + D_D, D_C + 2 * D_D], axis=-1)
    ucg = uc.astype(jnp.float32).reshape(Bsz, T, FNET_GROUPS, FNET_GROUP_DIM)
    y_c = jnp.fft.fft2(ucg, axes=(1, 3), norm="ortho").real
    y_c = y_c.reshape(Bsz, T, D_C).astype(h.dtype)
    y_d = gb * _dwconv_centred(gc * hs, sconv_w)
    return jnp.concatenate([y_c, y_d], axis=-1) @ w_out

def _channel_mixer(h, w_gate, w_up, conv_w, conv_b, w_down):
    g = _dwconv_centred(h @ w_gate, conv_w) + conv_b
    return (jax.nn.silu(g) * (h @ w_up)) @ w_down

def _trunk(x, c, ada_w, ada_b, norm_mix_g, norm_ffn_g, ffn_w_gate, ffn_w_up, ffn_conv_w, ffn_conv_b,
           ffn_w_down, ab_w_in, ab_w_out, s5_lam_re_f, s5_lam_im_f, s5_log_dt_f, s5_lam_re_b,
           s5_lam_im_b, s5_log_dt_b, s5_b_re, s5_b_im, s5_c_re, s5_c_im, s5_d, s5_w_glu, s5_b_glu,
           q_norm_g, k_norm_g, cd_w_in, cd_w_out, sconv_w):
    cond = jax.nn.silu(c)
    for layer in range(DEPTH):
        mod = cond @ ada_w[layer] + ada_b[layer]
        sh_m, sc_m, g_m, sh_f, sc_f, g_f = jnp.split(mod, 6, axis=-1)
        h = _modulate(_rms_norm(x, norm_mix_g[layer]), sh_m, sc_m)
        i = layer // 2
        if layer % 2 == 0:
            y = _mixer_ab(h, ab_w_in[i], ab_w_out[i], s5_lam_re_f[i], s5_lam_im_f[i], s5_log_dt_f[i],
                          s5_lam_re_b[i], s5_lam_im_b[i], s5_log_dt_b[i], s5_b_re[i], s5_b_im[i],
                          s5_c_re[i], s5_c_im[i], s5_d[i], s5_w_glu[i], s5_b_glu[i],
                          q_norm_g[i], k_norm_g[i])
        else:
            y = _mixer_cd(h, cd_w_in[i], cd_w_out[i], sconv_w[i])
        x = x + g_m[:, None, :] * y
        h = _modulate(_rms_norm(x, norm_ffn_g[layer]), sh_f, sc_f)
        x = x + g_f[:, None, :] * _channel_mixer(h, ffn_w_gate[layer], ffn_w_up[layer], ffn_conv_w[layer],
                                                 ffn_conv_b[layer], ffn_w_down[layer])
    return x

def setup_inputs(seed: int = 0) -> dict:
    key = jax.random.key(seed)
    ks = iter(jax.random.split(key, 40))

    def nrm(shape, scale):
        return jax.random.normal(next(ks), shape, jnp.float32) * scale

    n_idx = jnp.arange(S5_STATE, dtype=jnp.float32)
    lam_im0 = jnp.pi * n_idx

    def lam_re():
        return -0.5 + nrm((N_AB, S5_GROUPS, S5_STATE), 0.01)

    def lam_im():
        return lam_im0 + nrm((N_AB, S5_GROUPS, S5_STATE), 0.01)

    def log_dt():
        return jax.random.uniform(next(ks), (N_AB, S5_GROUPS), jnp.float32,
                                  minval=math.log(DT_MIN), maxval=math.log(DT_MAX))

    return {
        "x_prompt": nrm((BATCH, SEQ, D_MODEL), 1.0),
        "x_sample": nrm((DEC_BATCH, DEC_SEQ, D_MODEL), 1.0),
        "c_prompt": nrm((BATCH, D_MODEL), 1.0),
        "c_sample": nrm((DEC_BATCH, D_MODEL), 1.0),
        "ada_w": nrm((DEPTH, D_MODEL, 6 * D_MODEL), 0.5 * D_MODEL ** -0.5),
        "ada_b": nrm((DEPTH, 6 * D_MODEL), 0.01),
        "norm_mix_g": 1.0 + nrm((DEPTH, D_MODEL), 0.02),
        "norm_ffn_g": 1.0 + nrm((DEPTH, D_MODEL), 0.02),
        "ffn_w_gate": nrm((DEPTH, D_MODEL, D_FF), D_MODEL ** -0.5),
        "ffn_w_up": nrm((DEPTH, D_MODEL, D_FF), D_MODEL ** -0.5),
        "ffn_conv_w": nrm((DEPTH, CONV_W, D_FF), CONV_W ** -0.5),
        "ffn_conv_b": nrm((DEPTH, D_FF), 0.01),
        "ffn_w_down": nrm((DEPTH, D_FF, D_MODEL), D_FF ** -0.5),
        "ab_w_in": nrm((N_AB, D_MODEL, D_A + 3 * D_B), D_MODEL ** -0.5),
        "ab_w_out": nrm((N_AB, D_A + D_B, D_MODEL), (D_A + D_B) ** -0.5),
        "s5_lam_re_f": lam_re(),
        "s5_lam_im_f": lam_im(),
        "s5_log_dt_f": log_dt(),
        "s5_lam_re_b": lam_re(),
        "s5_lam_im_b": lam_im(),
        "s5_log_dt_b": log_dt(),
        "s5_b_re": nrm((N_AB, S5_GROUPS, S5_STATE, S5_GROUP), (2 * S5_GROUP) ** -0.5),
        "s5_b_im": nrm((N_AB, S5_GROUPS, S5_STATE, S5_GROUP), (2 * S5_GROUP) ** -0.5),
        "s5_c_re": nrm((N_AB, S5_GROUPS, S5_GROUP, S5_STATE), (2 * S5_STATE) ** -0.5),
        "s5_c_im": nrm((N_AB, S5_GROUPS, S5_GROUP, S5_STATE), (2 * S5_STATE) ** -0.5),
        "s5_d": nrm((N_AB, D_A), 1.0),
        "s5_w_glu": nrm((N_AB, D_A, D_A), D_A ** -0.5),
        "s5_b_glu": nrm((N_AB, D_A), 0.01),
        "q_norm_g": 1.0 + nrm((N_AB, HEAD_DIM), 0.02),
        "k_norm_g": 1.0 + nrm((N_AB, HEAD_DIM), 0.02),
        "cd_w_in": nrm((N_CD, D_MODEL, D_C + 3 * D_D), D_MODEL ** -0.5),
        "cd_w_out": nrm((N_CD, D_C + D_D, D_MODEL), (D_C + D_D) ** -0.5),
        "sconv_w": nrm((N_CD, CONV_W, D_D), CONV_W ** -0.5),
    }

def reference(x_prompt, x_sample, c_prompt, c_sample, ada_w, ada_b, norm_mix_g, norm_ffn_g,
              ffn_w_gate, ffn_w_up, ffn_conv_w, ffn_conv_b, ffn_w_down, ab_w_in, ab_w_out,
              s5_lam_re_f, s5_lam_im_f, s5_log_dt_f, s5_lam_re_b, s5_lam_im_b, s5_log_dt_b,
              s5_b_re, s5_b_im, s5_c_re, s5_c_im, s5_d, s5_w_glu, s5_b_glu, q_norm_g, k_norm_g,
              cd_w_in, cd_w_out, sconv_w):
    weights = (ada_w, ada_b, norm_mix_g, norm_ffn_g, ffn_w_gate, ffn_w_up, ffn_conv_w, ffn_conv_b,
               ffn_w_down, ab_w_in, ab_w_out, s5_lam_re_f, s5_lam_im_f, s5_log_dt_f, s5_lam_re_b,
               s5_lam_im_b, s5_log_dt_b, s5_b_re, s5_b_im, s5_c_re, s5_c_im, s5_d, s5_w_glu, s5_b_glu,
               q_norm_g, k_norm_g, cd_w_in, cd_w_out, sconv_w)
    y_prompt = _trunk(x_prompt, c_prompt, *weights)
    y_sample = _trunk(x_sample, c_sample, *weights)
    return (y_prompt, y_sample)


_drawn_inputs = setup_inputs


def setup_inputs(seed=0):
    import zlib

    import numpy as np

    out = dict(_drawn_inputs(seed))
    spreads = {}
    factors = {'ada_b': 3.281,
     'norm_mix_g': 5.749,
     'norm_ffn_g': 6.5,
     'ffn_conv_b': 22.715,
     's5_lam_re_f': 64.0,
     's5_lam_im_f': 64.0,
     's5_log_dt_f': 64.0,
     's5_lam_re_b': 64.0,
     's5_lam_im_b': 64.0,
     's5_log_dt_b': 64.0,
     's5_b_re': 59.624,
     's5_b_im': 64.0,
     's5_c_re': 63.296,
     's5_c_im': 64.0,
     's5_b_glu': 33.649,
     'q_norm_g': 8.0,
     'k_norm_g': 8.0}
    for name, (base, spread) in spreads.items():
        noise = np.random.default_rng([zlib.crc32(name.encode()), seed]).standard_normal(out[name].shape)
        drawn = base * np.exp(spread * noise) if base else spread * noise
        out[name] = __import__('jax').numpy.asarray(drawn.astype(out[name].dtype))
    for name, factor in factors.items():
        out[name] = (out[name] * factor).astype(out[name].dtype)
    return out
```

```python
import math
from contextlib import ExitStack

import numpy as np

import concourse.bass as bass
from concourse import mybir

F32 = mybir.dt.float32
F32R = mybir.dt.float32r
ALU = mybir.AluOpType
ACT = mybir.ActivationFunctionType

P = 128
D = 1024
KD = D // P
SEQ = (256, 512)
TOK = sum(SEQ)
TT = TOK // P
START = (0, SEQ[0])
HALF = TOK // 2
FF = 2816
FH = FF // P // 2
EPS = 1e-6
HEADS, HD = 8, 64
STEPS = 8
CH = 16
GRP = 32
PAIRS = GRP // 2
NCH = TOK // STEPS
CHUNKS = tuple(s // STEPS for s in SEQ)
MCH = max(CHUNKS)
PADDED = TOK + 3
MAGIC = 12582912.0
TWO_PI_HI, TWO_PI_MID = 6.28125, 0.0019350051879882812
TWO_PI_LO = 2 * math.pi - TWO_PI_HI - TWO_PI_MID
OVER = 3 * P

J_IN = (0, 88)
J_GLU = 16
J_OUT = (20, 104)
J_UP = ((28, 58), (112, 142))
J_DOWN = ((50, 80), (134, 164))
JOBS = 172


def depth(n):
    if J_GLU <= n < J_GLU + 4:
        return 4
    for layer in range(2):
        for first in J_DOWN[layer]:
            if first <= n < first + KD:
                return FH
    return KD


def build(nc, t, y_prompt, y_sample):
    ctx = ExitStack()
    with ctx:
        def sem(name):
            return ctx.enter_context(nc.semaphore(name))

        def sb(name, shape, dt=F32):
            return ctx.enter_context(nc.sbuf_tensor(name, shape, dt))

        xT = sb("xT", [P, KD, TOK])
        ident = sb("ident", [P, P])
        ones = sb("ones", [P, P])
        blk = sb("blk", [P, P])
        w_raw = [sb(f"w_raw{u}", [P, FH, P]) for u in range(2)]
        w_hi = [sb(f"w_hi{u}", [P, FH, P], F32R) for u in range(2)]
        w_lo = [sb(f"w_lo{u}", [P, FH, P], F32R) for u in range(2)]
        vecA = sb("vecA", [P, 128])
        vecB = sb("vecB", [P, 128])
        vecC = sb("vecC", [P, 128])
        mod = sb("mod", [P, 2, 48, 2])
        gain = sb("gain", [P, 2, 2, KD, 2])
        cond = sb("cond", [P, KD, 2])
        eps = sb("eps", [P, 1])
        att_l = sb("att_l", [P, 48])
        att_m = sb("att_m", [P, 48])
        att_nm = sb("att_nm", [P, 48])
        att_rl = sb("att_rl", [P, 48])
        bb = [[sb(f"bb{d}{r}", [P, PAIRS, CH]) for r in "ri"] for d in "fb"]
        ct = [sb(f"ct{r}", [P, PAIRS, CH]) for r in "rin"]
        powr = [sb(f"pow{r}", [P, 2, PAIRS, STEPS + 1]) for r in "ri"]
        stepA = sb("stepA", [P, 2, 2, 2, PAIRS])
        stepB = sb("stepB", [P, 2, 2, 2, PAIRS])
        ddiag = sb("ddiag", [CH, GRP, CH])

        origin = -(-nc.sbuf_base // 64) * 64
        arena_bytes = nc.sbuf_bytes_remaining // 64 * 64 - 64

        def at(name, kb, shape, dt=F32):
            size = int(np.prod(shape[1:])) * 4
            assert int(kb * 1024) + size <= arena_bytes, (name, kb, size, arena_bytes)
            return nc.alloc_sbuf_tensor_at(name, shape, dt, offset=origin + int(kb * 1024))

        xrows = at("xrows", 0, [P, TT, D])
        rowsA, rowsB, rowsC, rowsS = (at(f"rows{n}", 24 + i / 2, [P, P]) for i, n in enumerate("ABCS"))
        crow = [at(f"crow{r}", 26 + 2 * i, [P, 4, 2, 64]) for i, r in enumerate("ri")]
        braw = [at(f"braw{r}", 30 + i, [P, PAIRS, CH]) for i, r in enumerate("ri")]
        ldt = at("ldt", 32, [32, 2])
        s5v = at("s5v", 33, [P, 24, 32])
        drow = at("drow", 37, [CH, GRP, CH])
        s5t = [at(f"s5t{i}", 39 + i, [P, PAIRS, CH]) for i in range(2)]
        ada_w = [at(f"ada_w{s}", 48 + 16 * s, [P, KD, 512]) for s in range(4)]
        h_hi = at("h_hi", 0, [P, KD, TOK], F32R)
        h_lo = at("h_lo", 24, [P, KD, TOK], F32R)
        sq = [at(f"sq{i}", 100 + 3 * i, [P, TOK]) for i in range(2)]
        nt = [at(f"nt{i}", 106 + 3 * i, [P, TOK]) for i in range(2)]
        hf = [at(f"hf{i}", 112 + 3 * i, [P, TOK]) for i in range(2)]
        rstd = at("rstd", 118, [P, TOK])
        z0 = at("z0", 48, [P, 12, TOK])
        un = at("un", 84, [NCH, GRP, STEPS, CH])
        qsq = [at(f"qsq{i}", 118 + 3 * i, [P, TOK]) for i in range(2)]
        qr = [at(f"qr{i}", 124 + 3 * i, [P, TOK]) for i in range(2)]
        dist = at("dist", 0, [P, OVER + 512])
        lnc = at("lnc", 3.5, [P, OVER + 512])
        bias = [at(f"bias{i}", 7 + 3.5 * i, [P, OVER + 512]) for i in range(2)]
        att_s = [at(f"att_s{i}", 14 + 2 * i, [P, 512]) for i in range(2)]
        att_t = [at(f"att_t{i}", 18 + 2 * i, [P, 4, P]) for i in range(2)]
        yb = at("yb", 22, [P, TT, 512])
        vn = at("vn", 34, [P, TT, 512])
        mixb_hi = at("mixb_hi", 100, [P, 4, TOK], F32R)
        mixb_lo = at("mixb_lo", 112, [P, 4, TOK], F32R)
        uc = at("uc", 0, [P, GRP, NCH])
        XB = 2 * 2 * 2 * PAIRS
        xs = at("xs", 12, [P, MCH + 1, 2, 2, 2, PAIRS])
        rs = [[at(f"rs{d}{r}", 46 + 2 * (2 * d + r), [P, 4, STEPS, CH]) for r in range(2)] for d in range(2)]
        rt = at("rt", 54, [P, 4, 2, 2, 2, 64])
        s5tmp = [[at(f"s5tmp{d}{i}", 124 + 2.25 * (2 * d + i), [P, 4, STEPS + 1, CH]) for i in range(2)] for d in range(2)]
        scan = [at(f"scan{i}", 124 + i / 2, [P, XB]) for i in range(2)]
        cp = [[at(f"cp{d}{r}", 72 + 2.25 * (2 * d + r), [P, 4, STEPS + 1, CH]) for r in range(2)] for d in range(2)]
        kf = at("kf", 84, [CH, 8, 15 * CH])
        tm = at("tm", 92, [P, 8, P])
        yn = at("yn", 96, [NCH, STEPS, P])
        sp = at("sp", 46, [P, 2, 2, 4, NCH])
        ya = at("ya", 54, [P, 4, TOK])
        ya_hi = at("ya_hi", 12, [P, 4, TOK], F32R)
        ya_lo = at("ya_lo", 24, [P, 4, TOK], F32R)
        sig = [at(f"sig{i}", 36 + 3 * i, [P, TOK]) for i in range(2)]
        mixa_hi = at("mixa_hi", 66, [P, 4, TOK], F32R)
        mixa_lo = at("mixa_lo", 78, [P, 4, TOK], F32R)
        hid_hi = at("hid_hi", 48, [P, FH, TOK], F32R)
        hid_lo = at("hid_lo", 81, [P, FH, TOK], F32R)
        gpad = at("gpad", 114, [P, PADDED])
        conv = at("conv", 117.25, [P, PADDED])
        hidf = at("hidf", 120.5, [P, TOK])
        z1 = at("z1", 48, [P, 16, TOK])
        fv = at("fv", 0, [P, TT, 4, 256])
        dft = at("dft", 24, [P, 2, 4, 512])
        dftp = at("dftp", 40, [P, 2, 2, 256])
        cs = at("cs", 44, [P, 256])
        prod = at("prod", 124, [P, PADDED])
        pconv = at("pconv", 127.25, [P, PADDED])
        mixd_hi = at("mixd_hi", 100, [P, 4, TOK], F32R)
        mixd_lo = at("mixd_lo", 112, [P, 4, TOK], F32R)
        mixc_hi = at("mixc_hi", 60, [P, 4, TOK], F32R)
        mixc_lo = at("mixc_lo", 72, [P, 4, TOK], F32R)
        orow = [at(f"orow{i}", 4 * i, [P, D]) for i in range(TT)]

        pj = [ctx.enter_context(nc.psum_tensor(f"pj{u}", [P, 1024], F32)) for u in range(2)]
        pn = ctx.enter_context(nc.psum_tensor("pn", [P, 1024], F32))
        pa = ctx.enter_context(nc.psum_tensor("pa", [P, 512], F32))
        pb = ctx.enter_context(nc.psum_tensor("pb", [P, 512], F32))
        wide = slice(P, P + TOK)
        bank = [pj[0][:, 0:512], pj[0][:, 512:1024], pj[1][:, 0:512], pj[1][:, 512:1024]]

        kbank = ((pn[:, 0:512], pn[:, 512:1024]), (pa[:, :], pb[:, :]))

        const_in = sem("const_in"); x_in = sem("x_in"); rows_in = sem("rows_in"); s5_in = sem("s5_in")
        ada_in = [sem(f"ada_in{s}") for s in range(4)]
        mask_in = sem("mask_in"); dft_in = sem("dft_in"); t_in = sem("t_in"); out_done = sem("out_done")
        raw_in = [sem(f"raw_in{u}") for u in range(2)]
        w_hi_ready = sem("w_hi_ready"); w_lo_ready = sem("w_lo_ready"); job_done = sem("job_done")
        evac = [sem(f"evac{u}") for u in range(2)]
        v_seq = sem("v_seq"); a_seq = sem("a_seq"); g_seq = sem("g_seq")
        fill = sem("fill"); xt_ps = sem("xt_ps"); xt_ev = sem("xt_ev"); vec_ps = sem("vec_ps"); vec_ev = sem("vec_ev")
        c_ps = sem("c_ps"); expanded = sem("expanded"); cond_ready = sem("cond_ready"); ada_done = sem("ada_done")
        mod_ready = sem("mod_ready")
        s5a = sem("s5a"); s5b = sem("s5b"); s5d = sem("s5d")
        n_sq = sem("n_sq"); n_mm = sem("n_mm"); n_sd = sem("n_sd"); n_rs = sem("n_rs"); n_t = sem("n_t")
        n_hf = sem("n_hf"); n_hi = sem("n_hi"); h_ready = sem("h_ready")
        q_sq = sem("q_sq"); q_mm = sem("q_mm"); q_sd = sem("q_sd"); q_rc = sem("q_rc"); q_ready = sem("q_ready")
        v_tr = sem("v_tr"); v_ready = sem("v_ready")
        bias_half = sem("bias_half"); bias_ready = sem("bias_ready")
        a_s = sem("a_s"); a_m = sem("a_m"); a_nm = sem("a_nm"); a_p = sem("a_p"); a_t = sem("a_t")
        a_pt = sem("a_pt"); a_o = sem("a_o"); a_rl = sem("a_rl"); a_y = sem("a_y")
        yb_tr = sem("yb_tr"); yb_hi = sem("yb_hi"); yb_lo = sem("yb_lo")
        u_tr = sem("u_tr"); u_ev = sem("u_ev"); rs_f = sem("rs_f"); rs_b = sem("rs_b"); rt_tr = sem("rt_tr"); rt_ev = sem("rt_ev")
        r_mm = sem("r_mm"); r_ev = sem("r_ev"); x_zero = sem("x_zero")
        sc_mul = sem("sc_mul"); sc_add = sem("sc_add")
        cp_f = sem("cp_f"); cp_b = sem("cp_b"); k_mm = sem("k_mm"); k_ev = sem("k_ev"); sp_ready = sem("sp_ready")
        o_mm = sem("o_mm"); o_ev = sem("o_ev"); y_tr = sem("y_tr"); y_ev = sem("y_ev"); ya_h = sem("ya_h"); ya_l = sem("ya_l")
        glu_s = sem("glu_s"); glu_m = sem("glu_m"); glu_h = sem("glu_h"); glu_l = sem("glu_l")
        cv = sem("cv"); sl = sem("sl"); hh = sem("hh"); hl = sem("hl"); pad_zero = sem("pad_zero")
        gate0 = sem("gate0"); up0 = sem("up0")
        f_mm = sem("f_mm"); f_ev = sem("f_ev"); fy_mm = sem("fy_mm"); fy_hi = sem("fy_hi"); fy_lo = sem("fy_lo")
        d_seq = sem("d_seq"); d_f = sem("d_f"); d_h = sem("d_h"); d_l = sem("d_l")
        out_tr = sem("out_tr"); out_ev = sem("out_ev")

        block = ctx.enter_context(nc.Block())

        def wait_pos(eng, s, v):
            if not isinstance(v, int) or v > 0:
                eng.wait_ge(s, v)

        def pairs(eng, count, body):
            body(0)
            if count // 2 > 2:
                with eng.Fori(1, count // 2 - 1) as i:
                    body(i)
            body(count // 2 - 1)

        def ahead(first, i, u, own):
            return depth(first + 2 * i + u + 2) if isinstance(i, int) else own

        STAGES = []
        w_in = (t["ab_w_in"][0], t["cd_w_in"][0])
        w_out = (t["ab_w_out"][0], t["cd_w_out"][0])
        for layer in range(2):
            STAGES.append((J_IN[layer], 16, w_in[layer].rearrange("(k p) (j c) -> j p k c", p=P, c=P), None))
            if layer == 0:
                STAGES.append((J_GLU, 4, t["s5_w_glu"][0].rearrange("(k p) (j c) -> j p k c", p=P, c=P), None))
            STAGES.append((J_OUT[layer], KD, w_out[layer].rearrange("(k p) (j c) -> j p k c", p=P, c=P), None))
            for half in range(2):
                gate = t["ffn_w_gate"][layer].rearrange("(k p) (j c) -> j p k c", p=P, c=P)[half * FH:(half + 1) * FH]
                up = t["ffn_w_up"][layer].rearrange("(k p) (j c) -> j p k c", p=P, c=P)[half * FH:(half + 1) * FH]
                STAGES.append((J_UP[layer][half], 2 * FH, gate, up))
                down = t["ffn_w_down"][layer].rearrange("(h k p) (j c) -> h j p k c", h=2, p=P, c=P)[half]
                STAGES.append((J_DOWN[layer][half], KD, down, None))

        @block.sync
        def _(sp_e):
            sp_e.dma_start(ident[:, :], t["c_ident"]).then_inc(const_in, 16)
            sp_e.dma_start(blk[:, :], t["c_blk"]).then_inc(const_in, 16)
            for r in range(2):
                src = (t["x_prompt"], t["x_sample"])[r][0]
                sp_e.dma_start(xrows[:, START[r] // P:(START[r] + SEQ[r]) // P, :],
                               src.rearrange("(n p) d -> p n d", p=P)).then_inc(x_in, 16)
            for k in range(24):
                layer, j = divmod(k, 12)
                if k >= 4:
                    sp_e.wait_ge(ada_done, k - 3)
                sp_e.dma_start(ada_w[k % 4][:, :, :],
                               t["ada_w"][layer].rearrange("(k p) (j c) -> j p k c", p=P, c=512)[j]).then_inc(ada_in[k % 4], 16)
            for first, count, src, src2 in STAGES:
                def body(i, first=first, src=src, src2=src2):
                    for u in range(2):
                        wait_pos(sp_e, w_lo_ready, first + 2 * i + u - 1)
                        w = src2[i] if (src2 is not None and u) else src[i] if src2 is not None else src[2 * i + u]
                        sp_e.dma_start(w_raw[u][:, 0:depth(first), :], w).then_inc(raw_in[u], 16)
                if first == J_IN[0]:
                    body(0)
                    body(1)
                    with sp_e.Fori(2, count // 2 - 1) as i:
                        body(i)
                    body(count // 2 - 1)
                else:
                    pairs(sp_e, count, body)
                if first == J_GLU:
                    for q in range(4):
                        sp_e.wait_ge(k_ev, 4 * q + 4)
                        wait_pos(sp_e, o_mm, 2 * q)
                        for j in range(STEPS):
                            sp_e.dma_start(tm[CH * j:CH * j + CH, :, :],
                                           kf[:, :, (STEPS - 1 - j) * CH:(STEPS - 1 - j) * CH + P]).then_inc(t_in, 16)
                if first == J_IN[1]:
                    sp_e.wait_ge(job_done, J_IN[1] + 16)
                    for s in range(2):
                        sp_e.dma_start(dft[:, s, :, :], t["c_dft"][s].rearrange("(k p) n -> p k n", p=P)).then_inc(dft_in, 16)
                        sp_e.dma_start(dftp[:, s, :, :], t["c_dftp"][s].rearrange("(k p) n -> p k n", p=P)).then_inc(dft_in, 16)
                    sp_e.dma_start(cs[:, :], t["c_cs"]).then_inc(dft_in, 16)
            for n in range(TT):
                sp_e.wait_ge(out_ev, 2 * n + 2)
                dst = y_prompt[0] if n < 2 else y_sample[0]
                row = n * P if n < 2 else (n - 2) * P
                sp_e.dma_start(dst[row:row + P, :], orow[n][:, :]).then_inc(out_done, 16)
            sp_e.wait_ge(out_done, 16 * TT)

        @block.gpsimd
        def _(g):
            count = [0]

            def link(ins):
                count[0] += 1
                ins.then_inc(g_seq, 1)
                g.wait_ge(g_seq, count[0])

            nc.gpsimd.memset(ones[:, :], 1.0).then_inc(fill, 1)
            nc.gpsimd.memset(eps[:, :], EPS).then_inc(fill, 1)
            for tile in (rowsA, rowsB, rowsC, rowsS):
                link(nc.gpsimd.memset(tile[:, :], 0.0))
            rows = [
                (rowsA[0:16, :], t["norm_mix_g"].rearrange("l (k p) -> (l k) p", p=P)),
                (rowsA[16:32, :], t["norm_ffn_g"].rearrange("l (k p) -> (l k) p", p=P)),
                (rowsA[32:128, :], t["ada_b"].rearrange("l (k p) -> (l k) p", p=P)),
                (rowsB[0:66, :], t["ffn_conv_w"][0].rearrange("w (k p) -> (w k) p", p=P)),
                (rowsB[66:88, :], t["ffn_conv_b"][0].rearrange("(k p) -> k p", p=P)),
                (rowsB[88:92, :], t["s5_b_glu"][0].rearrange("(k p) -> k p", p=P)),
                (rowsB[92:104, :], t["sconv_w"][0].rearrange("w (k p) -> (w k) p", p=P)),
                (rowsB[104:112, :], t["c_prompt"][0].rearrange("(k p) -> k p", p=P)),
                (rowsB[112:120, :], t["c_sample"][0].rearrange("(k p) -> k p", p=P)),
                (rowsB[120:121, 0:64], t["q_norm_g"]), (rowsB[120:121, 64:128], t["q_norm_g"]),
                (rowsB[121:122, 0:64], t["k_norm_g"]), (rowsB[121:122, 64:128], t["k_norm_g"]),
                (rowsC[0:66, :], t["ffn_conv_w"][1].rearrange("w (k p) -> (w k) p", p=P)),
                (rowsC[66:88, :], t["ffn_conv_b"][1].rearrange("(k p) -> k p", p=P)),
                (rowsS[32:48, :], t["s5_lam_re_f"][0].rearrange("(k h) p -> k (h p)", h=2)),
                (rowsS[48:64, :], t["s5_lam_re_b"][0].rearrange("(k h) p -> k (h p)", h=2)),
                (rowsS[64:80, :], t["s5_lam_im_f"][0].rearrange("(k h) p -> k (h p)", h=2)),
                (rowsS[80:96, :], t["s5_lam_im_b"][0].rearrange("(k h) p -> k (h p)", h=2)),
                (ldt[0:16, :], t["s5_log_dt_f"][0].rearrange("(k h) -> k h", h=2)),
                (ldt[16:32, :], t["s5_log_dt_b"][0].rearrange("(k h) -> k h", h=2)),
            ]
            for dst, src in rows:
                g.dma_start(dst, src).then_inc(rows_in, 16)
            for r, (b, c) in enumerate((("s5_b_re", "s5_c_re"), ("s5_b_im", "s5_c_im"))):
                for h in range(2):
                    g.dma_start(braw[r][64 * h:64 * h + 64, :, :],
                                t[b][0].rearrange("(k h) p c -> h p k c", h=2)[h]).then_inc(s5_in, 16)
                    g.dma_start(crow[r][:, :, h, :],
                                t[c][0].rearrange("(k g) c p -> (g c) k p", g=8)).then_inc(s5_in, 16)
            g.dma_start(drow[:, :, :], t["s5_d"].rearrange("o (g c) -> o g c", c=CH).broadcast_to([CH, GRP, CH])
                        ).then_inc(s5_in, 16)
            assert len(rows) == 21
            g.wait_ge(job_done, J_IN[0] + 16)
            g.dma_start(dist[:, :], t["c_dist"]).then_inc(mask_in, 16)
            g.dma_start(lnc[:, :], t["c_lnc"]).then_inc(mask_in, 16)
            g.wait_ge(mask_in, 32)
            for h in range(HEADS):
                if h >= 2:
                    g.wait_ge(a_m, 6 * (h - 1))
                nc.gpsimd.tensor_scalar(bias[h % 2][:, :], dist[:, :], -(2.0 ** -(8.0 * (h + 1) / HEADS)), None,
                                        ALU.mult).then_inc(bias_half, 1)
                g.wait_ge(bias_half, h + 1)
                nc.gpsimd.tensor_tensor(bias[h % 2][:, :], bias[h % 2][:, :], lnc[:, :], ALU.add).then_inc(bias_ready, 1)
            g.wait_ge(yb_lo, 4)
            nc.gpsimd.memset(xs[:, :, :, :, :, :], 0.0).then_inc(x_zero, 1)
            for q in range(4):
                wait_pos(g, rt_tr, 4 * q)
                ks = slice(4 * q, 4 * q + 4)
                pr, pi = (powr[r][:, 1, ks, 0:STEPS].unsqueeze(3).broadcast_to([P, 4, STEPS, CH]) for r in range(2))
                br, bi = (bb[1][r][:, ks, :].unsqueeze(2).broadcast_to([P, 4, STEPS, CH]) for r in range(2))
                t1, t2 = (s5tmp[1][i][:, :, 0:STEPS, :] for i in range(2))
                link(nc.gpsimd.tensor_tensor(t1, pr, br, ALU.mult))
                link(nc.gpsimd.tensor_tensor(t2, pi, bi, ALU.mult))
                link(nc.gpsimd.tensor_tensor(rs[1][0][:, :, :, :], t1, t2, ALU.subtract))
                link(nc.gpsimd.tensor_tensor(t1, pr, bi, ALU.mult))
                link(nc.gpsimd.tensor_tensor(t2, pi, br, ALU.mult))
                nc.gpsimd.tensor_tensor(rs[1][1][:, :, :, :], t1, t2, ALU.add).then_inc(rs_b, 1)
                g.wait_ge(rs_b, q + 1)
            for q in range(4):
                wait_pos(g, o_mm, 2 * q)
                ks = slice(4 * q, 4 * q + 4)
                pr, pi = (powr[r][:, 1, ks, ::-1].unsqueeze(3).broadcast_to([P, 4, STEPS + 1, CH]) for r in range(2))
                cr, ci, cn = (ct[r][:, ks, :].unsqueeze(2).broadcast_to([P, 4, STEPS + 1, CH]) for r in range(3))
                t1, t2 = s5tmp[1][0][:, :, :, :], s5tmp[1][1][:, :, :, :]
                link(nc.gpsimd.tensor_tensor(t1, pr, cr, ALU.mult))
                link(nc.gpsimd.tensor_tensor(t2, pi, ci, ALU.mult))
                link(nc.gpsimd.tensor_tensor(cp[1][0][:, :, :, :], t1, t2, ALU.subtract))
                link(nc.gpsimd.tensor_tensor(t1, pi, cn, ALU.mult))
                link(nc.gpsimd.tensor_tensor(t2, pr, ci, ALU.mult))
                nc.gpsimd.tensor_tensor(cp[1][1][:, :, :, :], t1, t2, ALU.subtract).then_inc(cp_b, 1)
                g.wait_ge(cp_b, q + 1)
            for layer in range(2):
                g.wait_ge(h_ready, KD * (2 * layer + 2))
                for c in (0, SEQ[0] + 1, PADDED - 1):
                    nc.gpsimd.memset(gpad[:, c:c + 1], 0.0).then_inc(pad_zero, 1)
                if layer == 0:
                    g.wait_ge(h_ready, KD * 3)
                    for c in (0, SEQ[0] + 1, PADDED - 1):
                        nc.gpsimd.memset(prod[:, c:c + 1], 0.0).then_inc(pad_zero, 1)

        @block.scalar
        def _(a):
            count = [0]

            def link(ins):
                count[0] += 1
                ins.then_inc(a_seq, 1)
                a.wait_ge(a_seq, count[0])

            def next_split(first, i, u, own):
                n = first + 2 * i + u
                if isinstance(i, int) and n + 2 >= JOBS:
                    a.wait_ge(job_done, n + 1)
                    return
                k = ahead(first, i, u, own)
                a.wait_ge(job_done, n + 1)
                a.wait_ge(raw_in[u], 16 * (first // 2 + i + 2))
                nc.scalar.activation(w_hi[u][:, 0:k, :], w_raw[u][:, 0:k, :], ACT.Copy).then_inc(w_hi_ready, 1)

            a.wait_ge(fill, 2)
            a.wait_ge(vec_ev, 2)
            nc.scalar.activation(cond[:, :, :], vecB[:, 104:120].rearrange("p (r k) -> p k r", r=2), ACT.Silu).then_inc(cond_ready, 1)
            a.wait_ge(vec_ev, 4)
            nc.scalar.activation(s5v[:, 3, :], s5v[:, 0, :], ACT.Exp).then_inc(s5a, 1)
            a.wait_ge(s5d, 1)
            nc.scalar.activation(s5v[:, 5, :], s5v[:, 4, :], ACT.Exp).then_inc(s5a, 1)
            a.wait_ge(s5d, 2)
            nc.scalar.activation(s5v[:, 9, :], s5v[:, 8, :], ACT.Sin).then_inc(s5a, 1)
            nc.scalar.activation(s5v[:, 10, :], s5v[:, 8, :], ACT.Sin, scale=0.5).then_inc(s5a, 1)
            for u in range(2):
                a.wait_ge(raw_in[u], 16)
                nc.scalar.activation(w_hi[u][:, 0:KD, :], w_raw[u][:, 0:KD, :], ACT.Copy).then_inc(w_hi_ready, 1)

            def norm(k):
                layer, which = divmod(k, 2)
                for j in range(KD):
                    m = KD * k + j
                    wait_pos(a, n_mm, m - 1)
                    if m == 0:
                        a.wait_ge(xt_ev, 12)
                        a.wait_ge(ada_done, 24)
                    nc.scalar.activation(sq[j % 2][:, :], xT[:, j, :], ACT.Square).then_inc(n_sq, 1)
                a.wait_ge(n_mm, KD * (k + 1))
                nc.scalar.activation(rstd[:, :], pn[:, wide], ACT.Sqrt, bias=eps[:, 0:1], scale=1.0 / D).then_inc(n_sd, 1)
                a.wait_ge(mod_ready, 4)
                for j in range(KD):
                    m = KD * k + j
                    a.wait_ge(n_t, m + 1)
                    wait_pos(a, h_ready, m - 1)
                    for r in range(2):
                        s = slice(START[r], START[r] + SEQ[r])
                        nc.scalar.activation(hf[j % 2][:, s], nt[j % 2][:, s], ACT.Identity,
                                             bias=mod[:, layer, 24 * which + j, r:r + 1],
                                             scale=gain[:, layer, which, j, r:r + 1]).then_inc(n_hf, 1)
                    a.wait_ge(n_hf, 2 * m + 2)
                    nc.scalar.activation(h_hi[:, j, :], hf[j % 2][:, :], ACT.Copy).then_inc(n_hi, 1)

            def xwait(first):
                for u in range(2):
                    a.wait_ge(evac[u], first // 2)

            def out_stage(first, own, count):
                def body(i):
                    for u in range(2):
                        next_split(first, i, u, own)
                pairs(a, count, body)

            def ffn(layer):
                for half in range(2):
                    first = J_UP[layer][half]
                    seen = (2 * layer + half) * FH
                    a.wait_ge(pad_zero, 6 * layer + 3)

                    def body(i, first=first, seen=seen):
                        next_split(first, i, 0, KD)
                        wait_pos(a, cv, 3 * (seen + i))
                        nc.scalar.activation(gpad[:, 1:1 + SEQ[0]], pj[0][:, P:P + SEQ[0]], ACT.Copy).then_inc(gate0, 1)
                        nc.scalar.activation(gpad[:, 2 + SEQ[0]:2 + TOK], pj[0][:, P + SEQ[0]:P + TOK], ACT.Copy).then_inc(evac[0], 1)
                        next_split(first, i, 1, KD)
                        a.wait_ge(cv, 3 * (seen + i) + 3)
                        nc.scalar.activation(conv[:, 0:TOK + 1], conv[:, 0:TOK + 1], ACT.Silu).then_inc(sl, 1)
                        a.wait_ge(evac[1], first // 2 + i + 1)
                        nc.scalar.activation(hid_hi[:, i, :], hidf[:, :], ACT.Copy).then_inc(hh, 1)
                    if half == 0 and layer == 0:
                        body(0)
                        with a.Fori(1, FH - 1) as i:
                            body(i)
                        body(FH - 1)
                    else:
                        pairs(a, 2 * FH, body)
                    out_stage(J_DOWN[layer][half], FH, KD)

            norm(0)

            def ubody(i):
                for u in range(2):
                    next_split(0, i, u, KD)
                    src = pj[u][0:NCH, :].rearrange("n (j g c) -> n j g c", g=8, c=CH)
                    dst = un[:, 8 * (2 * i + u):8 * (2 * i + u) + 8, :, :].rearrange("n g j c -> n j g c")
                    nc.scalar.activation(dst, src, ACT.Copy).then_inc(evac[u], 1)
            ubody(0)
            ubody(1)

            def zbody(i):
                for u in range(2):
                    next_split(4, i, u, KD)
                    nc.scalar.activation(z0[:, 2 * i + u, :], pj[u][:, wide], ACT.Copy).then_inc(evac[u], 1)
            pairs(a, 12, zbody)
            for u in range(2):
                a.wait_ge(evac[u], 8)
            for k in range(8):
                wait_pos(a, q_mm, k - 1)
                nc.scalar.activation(qsq[k % 2][:, :], z0[:, k, :], ACT.Square).then_inc(q_sq, 1)
                a.wait_ge(q_mm, k + 1)
                wait_pos(a, q_ready, k - 1)
                nc.scalar.activation(qr[k % 2][:, :], pj[k % 2][:, wide], ACT.Sqrt, bias=eps[:, 0:1], scale=1.0 / HD).then_inc(q_sd, 1)

            def expo(n):
                a.wait_ge(a_nm, n + 1)
                w = SEQ[0] if n % TT < 2 else SEQ[1]
                nc.scalar.activation(att_s[n % 2][:, 0:w], att_s[n % 2][:, 0:w], ACT.Exp, bias=att_nm[:, n:n + 1],
                                     accum_out=att_l[:, n:n + 1]).then_inc(a_p, 1)
            expo(0)
            for n in range(48):
                if n < 47:
                    expo(n + 1)
                nk = (2 if n % TT < 2 else 4)
                a.wait_ge(a_t, n + 1)
                wait_pos(a, a_o, n - 1)
                nc.scalar.activation(att_t[n % 2][:, 0:nk, :], (pa, pb)[n % 2][:, 0:nk * P].rearrange("p (k q) -> p k q", q=P), ACT.Copy).then_inc(a_pt, 1)
            for k in range(4):
                a.wait_ge(yb_tr, k + 1)
                nc.scalar.activation(mixb_hi[:, k, :], pj[k % 2][:, wide], ACT.Copy).then_inc(yb_hi, 1)
            for q in range(4):
                for b in range(2):
                    a.wait_ge(u_tr, 2 * q + b + 1)
                    nc.scalar.activation(uc[:, 8 * q + 4 * b:8 * q + 4 * b + 4, :],
                                         bank[b][:, 0:4 * NCH].rearrange("p (g n) -> p g n", n=NCH), ACT.Copy).then_inc(u_ev, 1)
                wait_pos(a, r_mm, 4 * q)
                for b in range(4):
                    a.wait_ge(rt_tr, 4 * q + b + 1)
                    nc.scalar.activation(rt[:, :, :, b // 2, b % 2, :],
                                         bank[b][:, :].rearrange("p (k h s) -> p k h s", h=2, s=64), ACT.Copy).then_inc(rt_ev, 1)
            for q in range(4):
                wait_pos(a, o_mm, 2 * q)
                a.wait_ge(sc_add, 2 * (MCH - 1))
                ks = slice(4 * q, 4 * q + 4)
                for r in range(2):
                    m = CHUNKS[r]
                    c0 = START[r] // STEPS
                    for ri in range(2):
                        nc.scalar.activation(sp[:, 0, ri, :, c0:c0 + m], xs[:, 0:m, ri, 0, r, ks].rearrange("p m k -> p k m"),
                                             ACT.Copy).then_inc(sp_ready, 1)
                        nc.scalar.activation(sp[:, 1, ri, :, c0:c0 + m],
                                             xs[:, 0:m, ri, 1, r, ks][:, ::-1, :].rearrange("p m k -> p k m"),
                                             ACT.Copy).then_inc(sp_ready, 1)
                for b in range(2):
                    a.wait_ge(k_mm, 2 * q + b + 1)
                    wait_pos(a, t_in, 128 * q)
                    for h in range(2):
                        nc.scalar.activation(kf[:, 4 * b + h:4 * b + 4:2, :],
                                             kbank[b][h][0:CH, :].rearrange("p (g n) -> p g n", g=2)[:, :, 0:15 * CH],
                                             ACT.Copy).then_inc(k_ev, 1)
                for b in range(2):
                    a.wait_ge(o_mm, 2 * q + b + 1)
                    wait_pos(a, y_tr, 2 * q)
                    nc.scalar.activation(yn[:, :, :].rearrange("n i (g h c) -> n h g i c", h=2, c=CH)[:, b],
                                         bank[b][0:NCH, :].rearrange("n (g i c) -> n g i c", i=STEPS, c=CH),
                                         ACT.Gelu_apprx_tanh).then_inc(o_ev, 1)
            for k in range(4):
                a.wait_ge(y_ev, 2 * k + 2)
                nc.scalar.activation(ya_hi[:, k, :], ya[:, k, :], ACT.Copy).then_inc(ya_h, 1)
            for k in range(4):
                u = k % 2
                next_split(J_GLU, k // 2, u, 4)
                wait_pos(a, glu_m, k - 1)
                nc.scalar.activation(sig[u][:, :], pj[u][:, wide], ACT.Sigmoid, bias=vecB[:, 88 + k:89 + k]).then_inc(evac[u], 1)
                a.wait_ge(glu_m, k + 1)
                nc.scalar.activation(mixa_hi[:, k, :], sig[u][:, :], ACT.Copy).then_inc(glu_h, 1)
            out_stage(J_OUT[0], KD, KD)
            xwait(J_UP[0][0])
            norm(1)
            ffn(0)
            xwait(J_IN[1])
            norm(2)

            def z1body(i):
                for u in range(2):
                    next_split(J_IN[1], i, u, KD)
                    nc.scalar.activation(z1[:, 2 * i + u, :], pj[u][:, wide], ACT.Copy).then_inc(evac[u], 1)
            pairs(a, 16, z1body)
            for n in range(2 * TT):
                a.wait_ge(f_mm, n + 1)
                nc.scalar.activation(fv[:, n // 2, 2 * (n % 2):2 * (n % 2) + 2, :],
                                     bank[n % 4].rearrange("p (g c) -> p g c", g=2), ACT.Copy).then_inc(f_ev, 1)
            for k in range(4):
                a.wait_ge(d_f, k + 1)
                nc.scalar.activation(mixd_hi[:, k, :], pconv[:, 0:TOK], ACT.Copy).then_inc(d_h, 1)
            for k in range(4):
                a.wait_ge(fy_mm, k + 1)
                if k == 0:
                    a.wait_ge(d_l, 4)
                nc.scalar.activation(mixc_hi[:, k, :], pj[k % 2][:, wide], ACT.Copy).then_inc(fy_hi, 1)
            out_stage(J_OUT[1], KD, KD)
            xwait(J_UP[1][0])
            norm(3)
            ffn(1)

        @block.vector
        def _(v):
            count = [0]

            def link(ins):
                count[0] += 1
                ins.then_inc(v_seq, 1)
                v.wait_ge(v_seq, count[0])

            def tt(o, x, y, op):
                link(nc.vector.tensor_tensor(o, x, y, op))

            def low(n, u, k):
                v.wait_ge(w_hi_ready, n + 1)
                nc.vector.tensor_tensor(w_lo[u][:, 0:k, :], w_raw[u][:, 0:k, :], w_hi[u][:, 0:k, :].bitcast(F32),
                                        ALU.subtract).then_inc(w_lo_ready, 1)

            def next_low(first, i, u, own):
                if isinstance(i, int) and first + 2 * i + u + 2 >= JOBS:
                    return
                low(first + 2 * i + u + 2, u, ahead(first, i, u, own))

            for n in range(12):
                v.wait_ge(xt_ps, n + 1)
                nc.vector.tensor_copy(xT[:, 4 * (n % 2):4 * (n % 2) + 4, P * (n // 2):P * (n // 2) + P],
                                      bank[n % 4].rearrange("p (k c) -> p k c", k=4)).then_inc(xt_ev, 1)
            v.wait_ge(rows_in, 16 * 21)
            nc.vector.tensor_copy(rowsS[0:32, :].rearrange("p (h s) -> p h s", h=2),
                                  ldt[:, :].unsqueeze(2).broadcast_to([32, 2, 64])).then_inc(expanded, 1)
            v.wait_ge(vec_ps, 4)
            nc.vector.tensor_copy(vecA[:, :], pa[:, 0:128]).then_inc(vec_ev, 1)
            nc.vector.tensor_copy(vecB[:, :], pa[:, 128:256]).then_inc(vec_ev, 1)
            nc.vector.tensor_copy(vecC[:, :], pa[:, 256:384]).then_inc(vec_ev, 1)
            nc.vector.tensor_copy(s5v[:, 0:3, :], pa[:, 384:480].rearrange("p (k c) -> p k c", k=3)).then_inc(vec_ev, 1)
            v.wait_ge(vec_ev, 4)
            v.wait_ge(c_ps, 2)
            for r in range(2):
                src = (pb[:, :] if r == 0 else pn[:, 0:512]).rearrange("p (k h c) -> p k h c", h=2, c=CH)
                for h in range(2):
                    link(nc.vector.tensor_copy(ct[r][64 * h:64 * h + 64, :, :], src[64 * h:64 * h + 64, :, h, :]))
            link(nc.vector.tensor_scalar(ct[2][:, :, :], ct[0][:, :, :], -1.0, None, ALU.mult))
            link(nc.vector.tensor_scalar(vecB[:, 120:121], vecB[:, 120:121], 1.0 / math.sqrt(HD), None, ALU.mult))
            RE, IM, DT, MAG, TH, R, SIN, SH = (s5v[:, i, :] for i in (1, 2, 3, 5, 6, 8, 9, 10))
            T1, T2, T3, AR, AI, AM, CR, CI = (s5v[:, i, :] for i in (11, 12, 13, 14, 15, 16, 17, 18))
            v.wait_ge(s5a, 1)
            nc.vector.tensor_tensor(s5v[:, 4, :], RE, DT, ALU.mult).then_inc(s5d, 1)
            tt(TH, IM, DT, ALU.mult)
            link(nc.vector.tensor_scalar(T1, TH, 1.0 / (2 * math.pi), MAGIC, ALU.mult, ALU.add))
            link(nc.vector.tensor_scalar(T2, T1, -MAGIC, None, ALU.add))
            link(nc.vector.scalar_tensor_tensor(T1, T2, -TWO_PI_HI, TH, ALU.mult, ALU.add))
            link(nc.vector.scalar_tensor_tensor(T3, T2, -TWO_PI_MID, T1, ALU.mult, ALU.add))
            link(nc.vector.scalar_tensor_tensor(T1, T2, -TWO_PI_LO, T3, ALU.mult, ALU.add))
            nc.vector.tensor_scalar(R, T1, 3.1415925, -3.1415925, ALU.min, ALU.max).then_inc(s5d, 1)
            v.wait_ge(s5a, 4)
            tt(T1, SH, SH, ALU.mult)
            link(nc.vector.tensor_scalar(T2, T1, -2.0, 1.0, ALU.mult, ALU.add))
            tt(AR, MAG, T2, ALU.mult)
            tt(AI, MAG, SIN, ALU.mult)
            link(nc.vector.tensor_scalar(AM, AR, -1.0, None, ALU.add))
            tt(T1, RE, RE, ALU.mult)
            tt(T2, IM, IM, ALU.mult)
            tt(T3, T1, T2, ALU.add)
            link(nc.vector.reciprocal(T3, T3))
            tt(T1, AM, RE, ALU.mult)
            tt(T2, AI, IM, ALU.mult)
            tt(T1, T1, T2, ALU.add)
            tt(CR, T1, T3, ALU.mult)
            tt(T1, AI, RE, ALU.mult)
            tt(T2, AM, IM, ALU.mult)
            tt(T1, T1, T2, ALU.subtract)
            tt(CI, T1, T3, ALU.mult)
            v.wait_ge(s5_in, 16 * 9)
            for d in range(2):
                cr, ci = (x[:, PAIRS * d:PAIRS * d + PAIRS].unsqueeze(2).broadcast_to([P, PAIRS, CH]) for x in (CR, CI))
                x1, x2 = s5t[0][:, :, :], s5t[1][:, :, :]
                tt(x1, braw[0][:, :, :], cr, ALU.mult)
                tt(x2, braw[1][:, :, :], ci, ALU.mult)
                tt(bb[d][0][:, :, :], x1, x2, ALU.subtract)
                tt(x1, braw[1][:, :, :], cr, ALU.mult)
                tt(x2, braw[0][:, :, :], ci, ALU.mult)
                tt(bb[d][1][:, :, :], x1, x2, ALU.add)
            ar, ai = (x.rearrange("p (d k) -> p d k", d=2) for x in (AR, AI))
            t1, t2 = (x.rearrange("p (d k) -> p d k", d=2) for x in (T1, T2))
            link(nc.vector.memset(powr[0][:, :, :, 0], 1.0))
            link(nc.vector.memset(powr[1][:, :, :, 0], 0.0))
            for e in range(1, STEPS + 1):
                pr, pi = powr[0][:, :, :, e - 1], powr[1][:, :, :, e - 1]
                tt(t1, pr, ar, ALU.mult)
                tt(t2, pi, ai, ALU.mult)
                tt(powr[0][:, :, :, e], t1, t2, ALU.subtract)
                tt(t1, pr, ai, ALU.mult)
                tt(t2, pi, ar, ALU.mult)
                tt(powr[1][:, :, :, e], t1, t2, ALU.add)
            for r in range(2):
                for ri in range(2):
                    link(nc.vector.tensor_copy(stepA[:, ri, :, r, :], powr[0][:, :, :, STEPS]))
                link(nc.vector.tensor_scalar(stepB[:, 1, :, r, :], powr[1][:, :, :, STEPS], -1.0, None, ALU.mult))
                link(nc.vector.tensor_copy(stepB[:, 0, :, r, :], powr[1][:, :, :, STEPS]))
            v.wait_ge(const_in, 32)
            tt(ddiag[:, :, :], drow[:, :, :], ident[0:CH, 0:CH].unsqueeze(1).broadcast_to([CH, GRP, CH]), ALU.mult)
            for layer in range(2):
                v.wait_ge(ada_done, 12 * layer + 12)
                nc.vector.tensor_tensor(mod[:, layer, :, :], (pn[:, 512:608] if layer == 0 else pa[:, 0:96]).rearrange("p (k r) -> p k r", r=2),
                                        vecA[:, 32 + 48 * layer:80 + 48 * layer].unsqueeze(2).broadcast_to([P, 48, 2]),
                                        ALU.add).then_inc(s5b, 1)
                v.wait_ge(s5b, layer + 1)
                for which in range(2):
                    nc.vector.scalar_tensor_tensor(gain[:, layer, which, :, :], mod[:, layer, 24 * which + 8:24 * which + 16, :], 1.0,
                                                   vecA[:, 16 * which + 8 * layer:16 * which + 8 * layer + 8].unsqueeze(2).broadcast_to([P, KD, 2]),
                                                   ALU.add, ALU.mult).then_inc(mod_ready, 1)
            low(0, 0, KD)
            low(1, 1, KD)

            def norm(k):
                v.wait_ge(n_sd, k + 1)
                nc.vector.reciprocal(rstd[:, :], rstd[:, :]).then_inc(n_rs, 1)
                v.wait_ge(n_rs, k + 1)
                for j in range(KD + 1):
                    m = KD * k + j
                    if j < KD:
                        wait_pos(v, n_hf, 2 * (m - 1))
                        nc.vector.tensor_tensor(nt[j % 2][:, :], xT[:, j, :], rstd[:, :], ALU.mult).then_inc(n_t, 1)
                    if j:
                        v.wait_ge(n_hi, m)
                        nc.vector.tensor_tensor(h_lo[:, j - 1, :], hf[(j - 1) % 2][:, :], h_hi[:, j - 1, :].bitcast(F32),
                                                ALU.subtract).then_inc(h_ready, 1)

            def x_stage(layer, first, own, gate):
                def body(i):
                    for u in range(2):
                        next_low(first, i, u, own)
                        n = first + 2 * i + u
                        v.wait_ge(job_done, n + 1)
                        for r in range(2):
                            o = xT[:, 2 * i + u, START[r]:START[r] + SEQ[r]]
                            ins = nc.vector.scalar_tensor_tensor(o, pj[u][:, P + START[r]:P + START[r] + SEQ[r]],
                                                                 mod[:, layer, gate + 2 * i + u, r:r + 1], o, ALU.mult, ALU.add)
                            ins.then_inc((up0, evac[u])[r], 1)
                pairs(v, KD, body)

            def ffn(layer):
                vec = (vecB, vecC)[layer]
                for half in range(2):
                    first = J_UP[layer][half]
                    seen = (2 * layer + half) * FH

                    def body(i, first=first, seen=seen, half=half):
                        next_low(first, i, 0, KD)
                        f = half * FH + i
                        v.wait_ge(evac[0], first // 2 + i + 1)
                        n1 = TOK + 1
                        taps = [vec[:, 22 * w + f:22 * w + f + 1] for w in range(3)] if isinstance(f, int) else \
                               [vec[:, bass.ds(22 * w + f, 1)] for w in range(3)]
                        shift = vec[:, 66 + f:67 + f] if isinstance(f, int) else vec[:, bass.ds(66 + f, 1)]
                        nc.vector.tensor_scalar(conv[:, 0:n1], gpad[:, 1:1 + n1], taps[1], shift, ALU.mult, ALU.add).then_inc(cv, 1)
                        v.wait_ge(cv, 3 * (seen + i) + 1)
                        nc.vector.scalar_tensor_tensor(conv[:, 0:n1], gpad[:, 0:n1], taps[0], conv[:, 0:n1], ALU.mult, ALU.add).then_inc(cv, 1)
                        v.wait_ge(cv, 3 * (seen + i) + 2)
                        nc.vector.scalar_tensor_tensor(conv[:, 0:n1], gpad[:, 2:2 + n1], taps[2], conv[:, 0:n1], ALU.mult, ALU.add).then_inc(cv, 1)
                        next_low(first, i, 1, KD)
                        v.wait_ge(sl, seen + i + 1)
                        v.wait_ge(job_done, first + 2 * i + 2)
                        nc.vector.tensor_tensor(hidf[:, 0:SEQ[0]], conv[:, 0:SEQ[0]], pj[1][:, P:P + SEQ[0]], ALU.mult).then_inc(up0, 1)
                        nc.vector.tensor_tensor(hidf[:, SEQ[0]:TOK], conv[:, SEQ[0] + 1:TOK + 1], pj[1][:, P + SEQ[0]:P + TOK],
                                                ALU.mult).then_inc(evac[1], 1)
                        v.wait_ge(hh, seen + i + 1)
                        nc.vector.tensor_tensor(hid_lo[:, i, :], hidf[:, :], hid_hi[:, i, :].bitcast(F32), ALU.subtract).then_inc(hl, 1)
                    pairs(v, 2 * FH, body)
                    x_stage(layer, J_DOWN[layer][half], FH, 40)

            norm(0)

            def plain(first, cnt, own):
                def body(i):
                    for u in range(2):
                        next_low(first, i, u, own)
                pairs(v, cnt, body)
            plain(0, 16, KD)
            for b in range(6):
                v.wait_ge(v_tr, b + 1)
                nc.vector.tensor_copy(vn[:, b, :], bank[b % 4]).then_inc(v_ready, 1)
            for k in range(8):
                v.wait_ge(q_sd, k + 1)
                nc.vector.reciprocal(qr[k % 2][:, :], qr[k % 2][:, :]).then_inc(q_rc, 1)
                v.wait_ge(q_rc, k + 1)
                g = vecB[:, 120 + k // 4:121 + k // 4]
                nc.vector.scalar_tensor_tensor(z0[:, k, :], z0[:, k, :], g, qr[k % 2][:, :], ALU.mult, ALU.mult).then_inc(q_ready, 1)

            def scores(n):
                h, qt = divmod(n, TT)
                w = SEQ[0] if qt < 2 else SEQ[1]
                q0 = qt if qt < 2 else qt - 2
                v.wait_ge(a_s, n + 1)
                v.wait_ge(bias_ready, h + 1)
                wait_pos(v, a_t, n - 1)
                nc.vector.tensor_tensor_reduce(att_s[n % 2][:, 0:w], pn[:, 512 * (n % 2):512 * (n % 2) + w],
                                               bias[h % 2][:, OVER - P * q0:OVER - P * q0 + w], 1.0, -3.0e38,
                                               ALU.add, ALU.max, att_m[:, n:n + 1]).then_inc(a_m, 1)
                v.wait_ge(a_m, n + 1)
                nc.vector.tensor_scalar(att_nm[:, n:n + 1], att_m[:, n:n + 1], -1.0, None, ALU.mult).then_inc(a_nm, 1)
            scores(0)
            for n in range(48):
                if n < 47:
                    scores(n + 1)
                h, qt = divmod(n, TT)
                v.wait_ge(a_p, n + 1)
                nc.vector.reciprocal(att_rl[:, n:n + 1], att_l[:, n:n + 1]).then_inc(a_rl, 1)
                v.wait_ge(a_rl, n + 1)
                v.wait_ge(a_o, n + 1)
                nc.vector.tensor_scalar(yb[:, qt, HD * h:HD * h + HD], bank[n % 2][:, 0:HD],
                                        att_rl[:, n:n + 1], None, ALU.mult).then_inc(a_y, 1)
            for k in range(4):
                v.wait_ge(yb_hi, k + 1)
                nc.vector.tensor_tensor(mixb_lo[:, k, :], pj[k % 2][:, wide], mixb_hi[:, k, :].bitcast(F32), ALU.subtract).then_inc(yb_lo, 1)
            for q in range(4):
                wait_pos(v, rt_tr, 4 * q)
                ks = slice(4 * q, 4 * q + 4)
                pr, pi = (powr[r][:, 0, ks, 0:STEPS][:, :, ::-1].unsqueeze(3).broadcast_to([P, 4, STEPS, CH]) for r in range(2))
                br, bi = (bb[0][r][:, ks, :].unsqueeze(2).broadcast_to([P, 4, STEPS, CH]) for r in range(2))
                t1, t2 = (s5tmp[0][i][:, :, 0:STEPS, :] for i in range(2))
                tt(t1, pr, br, ALU.mult)
                tt(t2, pi, bi, ALU.mult)
                tt(rs[0][0][:, :, :, :], t1, t2, ALU.subtract)
                tt(t1, pr, bi, ALU.mult)
                tt(t2, pi, br, ALU.mult)
                nc.vector.tensor_tensor(rs[0][1][:, :, :, :], t1, t2, ALU.add).then_inc(rs_f, 1)
                v.wait_ge(rs_f, q + 1)
                v.wait_ge(x_zero, 1)
                for b in range(4):
                    k = 4 * q + b
                    v.wait_ge(r_mm, k + 1)
                    src = pn[:, 512 * (b % 2):512 * (b % 2) + 4 * NCH].rearrange("p (d r n) -> p d r n", d=2, r=2)
                    for d in range(2):
                        for r in range(2):
                            m, c0 = CHUNKS[r], START[r] // STEPS
                            part = src[:, d, :, c0:c0 + m]
                            if d:
                                part = part[:, :, ::-1]
                            ins = nc.vector.tensor_copy(xs[:, 1:1 + m, :, d, r, k].rearrange("p m r -> p r m"), part)
                            ins.then_inc(r_ev, 1)
            v.wait_ge(r_ev, 64)
            def flat(ap):
                return ap.rearrange("p r d q k -> p r (d q k)")
            with v.Fori(1, MCH) as m:
                prev = xs[:, m, :, :, :, :].rearrange("p r d q k -> p r (d q k)")
                new = xs[:, m + 1, :, :, :, :].rearrange("p r d q k -> p r (d q k)")
                s0, s1 = (scan[i][:, :].rearrange("p (r k) -> p r k", r=2) for i in range(2))
                nc.vector.tensor_tensor(s0, prev, flat(stepA[:, :, :, :, :]), ALU.mult).then_inc(sc_mul, 1)
                nc.vector.tensor_tensor(s1, prev, flat(stepB[:, :, :, :, :]), ALU.mult).then_inc(sc_mul, 1)
                v.wait_ge(sc_mul, 2 * m)
                nc.vector.tensor_tensor(new, new, s0, ALU.add).then_inc(sc_add, 1)
                v.wait_ge(sc_add, 2 * m - 1)
                nc.vector.tensor_tensor(new, new, s1[:, ::-1, :], ALU.add).then_inc(sc_add, 1)
                v.wait_ge(sc_add, 2 * m)
            for q in range(4):
                wait_pos(v, o_mm, 2 * q)
                ks = slice(4 * q, 4 * q + 4)
                pr, pi = (powr[r][:, 0, ks, :].unsqueeze(3).broadcast_to([P, 4, STEPS + 1, CH]) for r in range(2))
                cr, ci, cn = (ct[r][:, ks, :].unsqueeze(2).broadcast_to([P, 4, STEPS + 1, CH]) for r in range(3))
                t1, t2 = s5tmp[0][0][:, :, :, :], s5tmp[0][1][:, :, :, :]
                tt(t1, pr, cr, ALU.mult)
                tt(t2, pi, ci, ALU.mult)
                tt(cp[0][0][:, :, :, :], t1, t2, ALU.subtract)
                tt(t1, pi, cn, ALU.mult)
                tt(t2, pr, ci, ALU.mult)
                nc.vector.tensor_tensor(cp[0][1][:, :, :, :], t1, t2, ALU.subtract).then_inc(cp_f, 1)
                v.wait_ge(cp_f, q + 1)
                for b in range(2):
                    v.wait_ge(y_tr, 2 * q + b + 1)
                    src = (pa, pb)[b][:, 0:4 * NCH].rearrange("p (i n) -> p i n", i=4)
                    dst = ya[:, q, :].rearrange("p (n i) -> p i n", i=STEPS)[:, 4 * b:4 * b + 4, :]
                    nc.vector.tensor_copy(dst, src).then_inc(y_ev, 1)
            for k in range(4):
                v.wait_ge(ya_h, k + 1)
                nc.vector.tensor_tensor(ya_lo[:, k, :], ya[:, k, :], ya_hi[:, k, :].bitcast(F32), ALU.subtract).then_inc(ya_l, 1)
            for k in range(4):
                u = k % 2
                next_low(J_GLU, k // 2, u, 4)
                v.wait_ge(evac[u], (J_GLU + k) // 2 + 1)
                nc.vector.tensor_tensor(sig[u][:, :], sig[u][:, :], ya[:, k, :], ALU.mult).then_inc(glu_m, 1)
                v.wait_ge(glu_h, k + 1)
                nc.vector.tensor_tensor(mixa_lo[:, k, :], sig[u][:, :], mixa_hi[:, k, :].bitcast(F32), ALU.subtract).then_inc(glu_l, 1)
            x_stage(0, J_OUT[0], KD, 16)
            norm(1)
            ffn(0)
            norm(2)
            plain(J_IN[1], 16, KD)
            v.wait_ge(evac[0], J_OUT[1] // 2)
            v.wait_ge(evac[1], J_OUT[1] // 2)
            v.wait_ge(pad_zero, 6)
            n1 = TOK + 1
            seq = [0]

            def chain(ins):
                seq[0] += 1
                ins.then_inc(d_seq, 1)
                v.wait_ge(d_seq, seq[0])
            for k in range(4):
                gc, hs, gb = z1[:, 12 + k, :], z1[:, 4 + k, :], z1[:, 8 + k, :]
                taps = [vecB[:, 92 + 4 * w + k:93 + 4 * w + k] for w in range(3)]
                chain(nc.vector.tensor_tensor(prod[:, 1:1 + SEQ[0]], gc[:, 0:SEQ[0]], hs[:, 0:SEQ[0]], ALU.mult))
                chain(nc.vector.tensor_tensor(prod[:, 2 + SEQ[0]:2 + TOK], gc[:, SEQ[0]:TOK], hs[:, SEQ[0]:TOK], ALU.mult))
                chain(nc.vector.tensor_scalar(pconv[:, 0:n1], prod[:, 1:1 + n1], taps[1], None, ALU.mult))
                chain(nc.vector.scalar_tensor_tensor(pconv[:, 0:n1], prod[:, 0:n1], taps[0], pconv[:, 0:n1], ALU.mult, ALU.add))
                chain(nc.vector.scalar_tensor_tensor(pconv[:, 0:n1], prod[:, 2:2 + n1], taps[2], pconv[:, 0:n1], ALU.mult, ALU.add))
                chain(nc.vector.tensor_tensor(prod[:, 1:1 + SEQ[0]], pconv[:, 0:SEQ[0]], gb[:, 0:SEQ[0]], ALU.mult))
                chain(nc.vector.tensor_tensor(prod[:, 2 + SEQ[0]:2 + TOK], pconv[:, SEQ[0] + 1:n1], gb[:, SEQ[0]:TOK], ALU.mult))
                chain(nc.vector.tensor_copy(pconv[:, 0:SEQ[0]], prod[:, 1:1 + SEQ[0]]))
                nc.vector.tensor_copy(pconv[:, SEQ[0]:TOK], prod[:, 2 + SEQ[0]:2 + TOK]).then_inc(d_f, 1)
                v.wait_ge(d_h, k + 1)
                v.wait_ge(d_f, k + 1)
                nc.vector.tensor_tensor(mixd_lo[:, k, :], pconv[:, 0:TOK], mixd_hi[:, k, :].bitcast(F32), ALU.subtract).then_inc(d_l, 1)
            for k in range(4):
                v.wait_ge(fy_hi, k + 1)
                nc.vector.tensor_tensor(mixc_lo[:, k, :], pj[k % 2][:, wide], mixc_hi[:, k, :].bitcast(F32), ALU.subtract).then_inc(fy_lo, 1)
            x_stage(1, J_OUT[1], KD, 16)
            norm(3)
            ffn(1)
            for n in range(2 * TT):
                v.wait_ge(out_tr, n + 1)
                nc.vector.tensor_copy(orow[n // 2][:, 512 * (n % 2):512 * (n % 2) + 512], bank[n % 4]).then_inc(out_ev, 1)

        @block.tensor
        def _(pe):
            mm = nc.tensor.matmul

            def job(n, u, k, rhs_hi, rhs_lo, ready=None):
                pe.wait_ge(w_lo_ready, n + 1)
                for j in range(k):
                    if ready is not None:
                        pe.wait_ge(ready[0], ready[1] + j + 1)
                    for p, (w, x) in enumerate(((w_hi, rhs_hi), (w_hi, rhs_lo), (w_lo, rhs_hi))):
                        for c in range(2):
                            ins = mm(pj[u][:, P + c * HALF:P + (c + 1) * HALF], w[u][:, j, :], x(j)[:, c * HALF:(c + 1) * HALF],
                                     start=(j == 0 and p == 0), stop=(j == k - 1 and p == 2))
                ins.then_inc(job_done, 1)

            def jobs(first, cnt, k, rhs_hi, rhs_lo, ready=None):
                def body(i):
                    for u in range(2):
                        wait_pos(pe, evac[u], first // 2 + i)
                        job(first + 2 * i + u, u, k, rhs_hi, rhs_lo, ready if isinstance(i, int) and i == 0 and u == 0 else None)
                pairs(pe, cnt, body)

            pe.wait_ge(const_in, 32)
            pe.wait_ge(x_in, 32)
            for n in range(12):
                wait_pos(pe, xt_ev, n - 3)
                for k in range(4):
                    ins = nc.tensor.transpose(bank[n % 4][:, P * k:P * k + P],
                                              xrows[:, n // 2, P * (4 * (n % 2) + k):P * (4 * (n % 2) + k) + P], ident[:, :])
                ins.then_inc(xt_ps, 1)
            pe.wait_ge(rows_in, 16 * 21)
            pe.wait_ge(expanded, 1)
            for k, rows in enumerate((rowsA, rowsB, rowsC, rowsS)):
                nc.tensor.transpose(pa[:, P * k:P * k + P], rows[:, :], ident[:, :]).then_inc(vec_ps, 1)
            pe.wait_ge(s5_in, 16 * 9)
            for r in range(2):
                for k in range(4):
                    o = (pb if r == 0 else pn)[:, P * k:P * k + P]
                    ins = nc.tensor.transpose(o, crow[r][:, k, :, :].rearrange("p h s -> p (h s)"), ident[:, :])
                ins.then_inc(c_ps, 1)
            pe.wait_ge(cond_ready, 1)
            pe.wait_ge(vec_ev, 4)
            for k in range(24):
                pe.wait_ge(ada_in[k % 4], 16 * (k // 4 + 1))
                for s in range(4):
                    c = 2 * (4 * (k % 12) + s)
                    o = pn[:, 512 + c:514 + c] if k < 12 else pa[:, c:c + 2]
                    for j in range(KD):
                        ins = mm(o, ada_w[k % 4][:, j, P * s:P * s + P], cond[:, j, :], start=(j == 0), stop=(j == KD - 1))
                ins.then_inc(ada_done, 1)

            def norm(k, first):
                pe.wait_ge(fill, 2)
                for j in range(KD):
                    pe.wait_ge(n_sq, KD * k + j + 1)
                    if j == 0:
                        pe.wait_ge(mod_ready, 4)
                    for c in range(2):
                        ins = mm(pn[:, P + c * HALF:P + (c + 1) * HALF], ones[:, :], sq[j % 2][:, c * HALF:(c + 1) * HALF],
                                 start=(j == 0), stop=(j == KD - 1))
                    ins.then_inc(n_mm, 1)

            def h_parts(j):
                return h_hi[:, j, :]

            def l_parts(j):
                return h_lo[:, j, :]

            norm(0, 0)
            for n in range(4):
                u = n % 2
                wait_pos(pe, evac[u], n // 2)
                pe.wait_ge(w_lo_ready, n + 1)
                for j in range(STEPS):
                    for k in range(KD):
                        if n == 0 and j == 0:
                            pe.wait_ge(h_ready, k + 1)
                        for p, (x, w) in enumerate(((h_hi, w_hi), (h_lo, w_hi), (h_hi, w_lo))):
                            ins = mm(pj[u][0:NCH, P * j:P * j + P], x[:, k, j:TOK:STEPS], w[u][:, k, :],
                                     start=(k == 0 and p == 0), stop=(k == KD - 1 and p == 2))
                ins.then_inc(job_done, 1)
            jobs(4, 12, KD, h_parts, l_parts)
            for u in range(2):
                pe.wait_ge(evac[u], 8)
            for b in range(6):
                wait_pos(pe, v_ready, b - 3)
                for k in range(4):
                    ins = nc.tensor.transpose(bank[b % 4][:, P * k:P * k + P], z0[:, 8 + k, P * b:P * b + P], ident[:, :])
                ins.then_inc(v_tr, 1)
            pe.wait_ge(v_ready, 6)
            for k in range(8):
                pe.wait_ge(q_sq, k + 1)
                wait_pos(pe, q_sd, k - 1)
                for c in range(2):
                    ins = mm(pj[k % 2][:, P + c * HALF:P + (c + 1) * HALF], blk[:, :], qsq[k % 2][:, c * HALF:(c + 1) * HALF],
                             start=True, stop=True)
                ins.then_inc(q_mm, 1)
            pe.wait_ge(q_ready, 8)

            def geo(n):
                h, qt = divmod(n, TT)
                r = 0 if qt < 2 else 1
                return h, qt, START[r], SEQ[r]

            def score(n):
                h, qt, k0, w = geo(n)
                wait_pos(pe, a_m, n - 1)
                rows = slice(HD * (h % 2), HD * (h % 2) + HD)
                mm(pn[:, 512 * (n % 2):512 * (n % 2) + w], z0[rows, h // 2, P * qt:P * qt + P], z0[rows, 4 + h // 2, k0:k0 + w],
                   start=True, stop=True).then_inc(a_s, 1)
            score(0)
            for n in range(48):
                if n < 47:
                    score(n + 1)
                h, qt, k0, w = geo(n)
                pe.wait_ge(a_p, n + 1)
                wait_pos(pe, a_pt, n - 1)
                for k in range(w // P):
                    ins = nc.tensor.transpose((pa, pb)[n % 2][:, P * k:P * k + P], att_s[n % 2][:, P * k:P * k + P], ident[:, :])
                ins.then_inc(a_t, 1)
                pe.wait_ge(a_pt, n + 1)
                wait_pos(pe, a_y, n - 1)
                for k in range(w // P):
                    ins = mm(bank[n % 2][:, 0:HD], att_t[n % 2][:, k, :], vn[:, k0 // P + k, HD * h:HD * h + HD],
                             start=(k == 0), stop=(k == w // P - 1))
                ins.then_inc(a_o, 1)
            pe.wait_ge(a_y, 48)
            for k in range(4):
                wait_pos(pe, yb_lo, k - 1)
                for b in range(TT):
                    ins = nc.tensor.transpose(pj[k % 2][:, P + P * b:P + P * b + P], yb[:, b, P * k:P * k + P], ident[:, :])
                ins.then_inc(yb_tr, 1)
            pe.wait_ge(yb_lo, 4)
            for q in range(4):
                wait_pos(pe, rt_ev, 4 * q)
                for b in range(2):
                    for g in range(4):
                        ins = nc.tensor.transpose(bank[b][:, NCH * g:NCH * g + NCH],
                                                  un[:, 8 * q + 4 * b + g, :, :].rearrange("n j c -> n (j c)"), ident[0:NCH, 0:NCH])
                    ins.then_inc(u_tr, 1)
                pe.wait_ge(u_ev, 2 * q + 2)
                pe.wait_ge(rs_f, q + 1)
                pe.wait_ge(rs_b, q + 1)
                for b in range(4):
                    for k in range(4):
                        ins = nc.tensor.transpose(bank[b][:, P * k:P * k + P],
                                                  rs[b // 2][b % 2][:, k, :, :].rearrange("p j c -> p (j c)"), ident[:, :])
                    ins.then_inc(rt_tr, 1)
                pe.wait_ge(rt_ev, 4 * q + 4)
                for k in range(4):
                    wait_pos(pe, r_ev, 4 * (4 * q + k - 1))
                    for d in range(4):
                        for h in range(2):
                            ins = mm(pn[64 * h:64 * h + 64, 512 * (k % 2) + NCH * d:512 * (k % 2) + NCH * (d + 1)],
                                     rt[:, k, h, d // 2, d % 2, :], uc[:, 8 * q + 2 * k + h, :], start=True, stop=True)
                    ins.then_inc(r_mm, 1)
            for q in range(4):
                pe.wait_ge(cp_f, q + 1)
                pe.wait_ge(cp_b, q + 1)
                if q == 0:
                    pe.wait_ge(r_ev, 64)
                for b in range(2):
                    wait_pos(pe, k_ev, 4 * q)
                    wait_pos(pe, y_ev, 2 * q)
                    for k in range(2 * b, 2 * b + 2):
                        for h in range(2):
                            rows = slice(64 * h, 64 * h + 64)
                            o = kbank[b][h][0:CH, 256 * (k % 2):256 * (k % 2) + 256]
                            for d, c0, j0 in ((1, 0, 1), (0, 7 * CH, 0)):
                                for r in range(2):
                                    mm(o[:, c0:c0 + P], bb[d][r][rows, 4 * q + k, :],
                                       cp[d][r][rows, k, j0:j0 + STEPS, :].rearrange("p j c -> p (j c)"),
                                       start=(d == 1 and r == 0), stop=False, skip_group_check=True)
                            ins = mm(o[:, 7 * CH:8 * CH], ident[0:CH, 0:CH], ddiag[:, 8 * q + 2 * k + h, :],
                                     start=False, stop=True, skip_group_check=True)
                    ins.then_inc(k_mm, 1)
                pe.wait_ge(sp_ready, 8 * q + 8)
                pe.wait_ge(t_in, 128 * (q + 1))
                for b in range(2):
                    wait_pos(pe, o_ev, 2 * q)
                    for k in range(4):
                        rows = slice(64 * b, 64 * b + 64)
                        o = bank[b][0:NCH, P * k:P * k + P]
                        mm(o, uc[:, 8 * q + 2 * k + b, :], tm[:, 2 * k + b, :], start=True, stop=False)
                        for d in range(2):
                            for r in range(2):
                                ins = mm(o, sp[rows, d, r, k, :],
                                         cp[d][r][rows, k, 1 - d:1 - d + STEPS, :].rearrange("p j c -> p (j c)"),
                                         start=False, stop=(d == 1 and r == 1))
                    ins.then_inc(o_mm, 1)
                pe.wait_ge(o_ev, 2 * q + 2)
                for b in range(2):
                    wait_pos(pe, y_ev, 2 * q)
                    for i in range(4):
                        ins = nc.tensor.transpose((pa, pb)[b][:, NCH * i:NCH * i + NCH], yn[:, 4 * b + i, :], ident[0:NCH, 0:NCH])
                    ins.then_inc(y_tr, 1)
            jobs(J_GLU, 4, 4, lambda j: ya_hi[:, j, :], lambda j: ya_lo[:, j, :], (ya_l, 0))
            pe.wait_ge(glu_l, 4)
            jobs(J_OUT[0], KD, KD, lambda j: (mixa_hi if j < 4 else mixb_hi)[:, j % 4, :],
                 lambda j: (mixa_lo if j < 4 else mixb_lo)[:, j % 4, :])

            def ffn(layer):
                norm(2 * layer + 1, J_UP[layer][0])
                for half in range(2):
                    jobs(J_UP[layer][half], 2 * FH, KD, h_parts, l_parts, (h_ready, KD * (2 * layer + 1)) if half == 0 else None)
                    jobs(J_DOWN[layer][half], KD, FH, lambda j: hid_hi[:, j, :], lambda j: hid_lo[:, j, :],
                         (hl, FH * (2 * layer + half)))
            ffn(0)
            norm(2, J_IN[1])
            jobs(J_IN[1], 16, KD, h_parts, l_parts, (h_ready, 2 * KD))
            pe.wait_ge(dft_in, 16 * 5)
            for u in range(2):
                pe.wait_ge(evac[u], J_OUT[1] // 2)
            for n in range(2 * TT):
                wait_pos(pe, f_ev, n - 3)
                for s in range(2):
                    ins = mm(bank[n % 4][:, 256 * s:256 * s + 256], z1[:, 2 * (n % 2) + s, P * (n // 2):P * (n // 2) + P], cs[:, :],
                             start=True, stop=True)
                ins.then_inc(f_mm, 1)
            pe.wait_ge(f_ev, 2 * TT)
            for k in range(4):
                wait_pos(pe, fy_lo, k - 1)
                u = k % 2
                for s in range(2):
                    for b in range(2):
                        mm(pj[u][:, P:P + SEQ[0]], fv[:, b, k, P * s:P * s + P], dftp[:, s, b, :],
                           start=(s == 0 and b == 0), stop=(s == 1 and b == 1))
                for c0, c1 in ((0, 128), (128, 512)):
                    for s in range(2):
                        for b in range(4):
                            ins = mm(pj[u][:, P + SEQ[0] + c0:P + SEQ[0] + c1], fv[:, 2 + b, k, P * s:P * s + P], dft[:, s, b, c0:c1],
                                     start=(s == 0 and b == 0), stop=(s == 1 and b == 3))
                ins.then_inc(fy_mm, 1)
            pe.wait_ge(d_l, 4)
            pe.wait_ge(fy_lo, 4)
            jobs(J_OUT[1], KD, KD, lambda j: (mixc_hi if j < 4 else mixd_hi)[:, j % 4, :],
                 lambda j: (mixc_lo if j < 4 else mixd_lo)[:, j % 4, :])
            ffn(1)
            for u in range(2):
                pe.wait_ge(evac[u], JOBS // 2)
            for n in range(2 * TT):
                wait_pos(pe, out_ev, n - 3)
                for k in range(4):
                    ins = nc.tensor.transpose(bank[n % 4][:, P * k:P * k + P], xT[:, 4 * (n % 2) + k, P * (n // 2):P * (n // 2) + P],
                                              ident[:, :])
                ins.then_inc(out_tr, 1)


INS = ["x_prompt", "x_sample", "c_prompt", "c_sample", "ada_w", "ada_b", "norm_mix_g", "norm_ffn_g", "ffn_w_gate",
       "ffn_w_up", "ffn_conv_w", "ffn_conv_b", "ffn_w_down", "ab_w_in", "ab_w_out", "s5_lam_re_f", "s5_lam_im_f",
       "s5_log_dt_f", "s5_lam_re_b", "s5_lam_im_b", "s5_log_dt_b", "s5_b_re", "s5_b_im", "s5_c_re", "s5_c_im", "s5_d",
       "s5_w_glu", "s5_b_glu", "q_norm_g", "k_norm_g", "cd_w_in", "cd_w_out", "sconv_w"]


def constants():
    head = np.kron(np.eye(P // HD), np.ones((HD, HD)))
    d = np.arange(P)[:, None] - (np.arange(OVER + 512)[None, :] - OVER)
    dist = np.abs(d)
    branches = sum(((dist % dil == 0) & (dist <= win // 2)).astype(np.int64) for win, dil in ((128, 1), (512, 4), (2048, 16)))
    lnc = np.where(branches > 0, np.log(np.maximum(branches, 1)), -1e30)

    def fourier(n):
        a = 2 * np.pi * (np.outer(np.arange(n), np.arange(n)) % n) / n
        return np.cos(a) / math.sqrt(n), np.sin(a) / math.sqrt(n)
    c, s = fourier(P)
    big, small = fourier(SEQ[1]), fourier(SEQ[0])
    out = {"c_ident": np.eye(P), "c_blk": head, "c_dist": dist, "c_lnc": lnc, "c_cs": np.concatenate([c, s], 1),
           "c_dft": np.stack([big[0], -big[1]]), "c_dftp": np.stack([small[0], -small[1]])}
    return {k: np.ascontiguousarray(v, dtype=np.float32) for k, v in out.items()}


def kernel(**inputs):
    import concourse.bacc as bacc
    from concourse.bass_utils import run_bass_kernel_spmd

    nc = bacc.Bacc("TRN2", target_bir_lowering=False, num_devices=1)
    arrays, tensors = {}, {}
    for name, a in [(n, inputs[n]) for n in INS] + list(constants().items()):
        a = np.ascontiguousarray(a)
        arrays["in_" + name] = a
        tensors[name] = nc.dram_tensor("in_" + name, a.shape, mybir.dt.from_np(a.dtype), kind="ExternalInput").ap()
    outs = [nc.dram_tensor(n, (1, s, D), F32, kind="ExternalOutput").ap() for n, s in (("y_prompt", SEQ[0]), ("y_sample", SEQ[1]))]
    build(nc, tensors, *outs)
    r = run_bass_kernel_spmd(nc, [arrays], core_ids=[0])
    return r.results[0]["y_prompt"], r.results[0]["y_sample"]
```

```python
import math
from contextlib import ExitStack

import numpy as np

import concourse.bass as bass
from concourse import mybir

F32 = mybir.dt.float32
F32R = mybir.dt.float32r
ALU = mybir.AluOpType
ACT = mybir.ActivationFunctionType

P = 128
D = 1024
KD = D // P
SEQ = (256, 512)
TOK = sum(SEQ)
TT = TOK // P
START = (0, SEQ[0])
HALF = TOK // 2
FF = 2816
FH = FF // P // 2
EPS = 1e-6
HEADS, HD = 8, 64
STEPS = 8
CH = 16
GRP = 32
PAIRS = GRP // 2
NCH = TOK // STEPS
CHUNKS = tuple(s // STEPS for s in SEQ)
MCH = max(CHUNKS)
PADDED = TOK + 3
MAGIC = 12582912.0
TWO_PI_HI, TWO_PI_MID = 6.28125, 0.0019350051879882812
TWO_PI_LO = 2 * math.pi - TWO_PI_HI - TWO_PI_MID
ADA = 256
QG = 104
ROW_DMAS = 19
OVER = 3 * P

J_IN = (0, 88)
J_GLU = 16
J_OUT = (20, 104)
J_UP = ((28, 58), (112, 142))
J_DOWN = ((50, 80), (134, 164))
JOBS = 172


def depth(n):
    if J_GLU <= n < J_GLU + 4:
        return 4
    for layer in range(2):
        for first in J_DOWN[layer]:
            if first <= n < first + KD:
                return FH
    return KD


def build(nc, t, y_prompt, y_sample):
    ctx = ExitStack()
    with ctx:
        def sem(name):
            return ctx.enter_context(nc.semaphore(name))

        def sb(name, shape, dt=F32):
            return ctx.enter_context(nc.sbuf_tensor(name, shape, dt))

        xT = sb("xT", [P, KD, TOK])
        ident = sb("ident", [P, P])
        ones = sb("ones", [P, 1])
        blk = sb("blk", [P, 2])
        w_raw = [sb(f"w_raw{u}", [P, FH, P]) for u in range(2)]
        w_hi = [sb(f"w_hi{u}", [P, FH, P], F32R) for u in range(2)]
        w_lo = [sb(f"w_lo{u}", [P, FH, P], F32R) for u in range(2)]
        vecA = sb("vecA", [P, 128])
        vecB = sb("vecB", [P, 128])
        vecC = sb("vecC", [P, 128])
        mod = sb("mod", [P, 2, 48, 2])
        gain = sb("gain", [P, 2, 2, KD, 2])
        cond = sb("cond", [P, KD, 2])
        eps = sb("eps", [P, 1])
        att_l = sb("att_l", [P, 48])
        att_m = sb("att_m", [P, 48])
        att_nm = sb("att_nm", [P, 48])
        att_rl = sb("att_rl", [P, 48])
        bb = [[sb(f"bb{d}{r}", [P, PAIRS, CH]) for r in "ri"] for d in "fb"]
        ct = [sb(f"ct{r}", [P, PAIRS, CH]) for r in "rin"]
        powr = [sb(f"pow{r}", [P, 2, PAIRS, STEPS + 1]) for r in "ri"]
        stepA = sb("stepA", [P, 2, 2, 2, PAIRS])
        stepB = sb("stepB", [P, 2, 2, 2, PAIRS])
        ddiag = sb("ddiag", [CH, GRP, CH])
        pick = sb("pick", [P, 2, 2])
        rms = sb("rms", [P, TT])
        qrms = sb("qrms", [P, TT, 2 * HEADS])

        origin = -(-nc.sbuf_base // 64) * 64
        arena_bytes = nc.sbuf_bytes_remaining // 64 * 64 - 64

        def at(name, kb, shape, dt=F32):
            size = int(np.prod(shape[1:])) * 4
            assert int(kb * 1024) + size <= arena_bytes, (name, kb, size, arena_bytes)
            return nc.alloc_sbuf_tensor_at(name, shape, dt, offset=origin + int(kb * 1024))

        xrows = at("xrows", 0, [P, TT, D])
        rowsA, rowsB, rowsC, rowsS = (at(f"rows{n}", 24 + i / 2, [P, P]) for i, n in enumerate("ABCS"))
        crows = at("crows", 26, [2 * KD, P])
        ldt = at("ldt", 32, [32, 2])
        drow = at("drow", 41, [CH, GRP, CH])
        mod_row = [at(f"mod_row{i}", 43 + 2 * i, [2, 512]) for i in range(2)]
        ada_a = [at(f"ada_a{i}", 48 + 16 * i, [P, KD, 512]) for i in range(3)]
        s5v = at("s5v", 114, [P, 24, 32])
        braw = [at(f"braw{r}", 117 + i, [P, PAIRS, CH]) for i, r in enumerate("ri")]
        s5t = [at(f"s5t{i}", 119 + i, [P, PAIRS, CH]) for i in range(2)]
        crow = [at(f"crow{r}", 121 + 2 * i, [P, 4, 2, 64]) for i, r in enumerate("ri")]
        ada_w = [at(f"ada_w{i}", 125 + 4 * i, [P, KD // 2, ADA]) for i in range(2)]
        ada_acc0 = [at(f"ada_acc{r}", 108 + r, [P, ADA]) for r in range(2)]
        ada_row0 = at("ada_row", 110, [2, ADA])
        h_hi = at("h_hi", 0, [P, KD, TOK], F32R)
        h_lo = at("h_lo", 24, [P, KD, TOK], F32R)
        sq_first = [at(f"sq_first{i}", 96 + 3 * i, [P, TOK]) for i in range(2)]
        sq_later = [at(f"sq_later{i}", 125 + 3 * i, [P, TOK]) for i in range(2)]
        sq_acc = at("sq_acc", 131, [P, TOK])
        nt = [at(f"nt{i}", 102 + 3 * i, [P, TOK]) for i in range(2)]
        hf = [at(f"hf{i}", 108 + 3 * i, [P, TOK]) for i in range(2)]
        z0 = at("z0", 48, [P, 12, TOK])
        un = at("un", 84, [NCH, GRP, STEPS, CH])
        ut = [at(f"ut{i}", 102 + 3 * i, [P, TOK]) for i in range(2)]
        qsq = [at(f"qsq{i}", 114 + 3 * i, [P, TOK]) for i in range(2)]
        q_rows = at("q_rows", 120, [2 * HEADS, TOK])
        spread = at("spread", 126, [2 * HEADS, 8, P])
        uc = at("uc", 0, [P, GRP, NCH])
        xs = at("xs", 12, [P, MCH + 1, 2, 2, 2, PAIRS])
        rs = [[at(f"rs{d}{r}", 100 + 2 * (2 * d + r), [P, 4, STEPS, CH]) for r in range(2)] for d in range(2)]
        scan = [at(f"scan{i}", 44.5 + i / 2, [P, 2 * 2 * 2 * PAIRS]) for i in range(2)]
        rt = at("rt", 115, [P, 4, 2, 2, 2, 64])
        rtmp = [[at(f"rtmp{d}{i}", (45.5, 127, 129, 131)[2 * d + i], [P, 4, STEPS, CH]) for i in range(2)] for d in range(2)]
        dist = at("dist", 108, [P, OVER + 512])
        lnc = at("lnc", 111.5, [P, OVER + 512])
        bias = [at(f"bias{i}", 84 + 3.5 * i, [P, OVER + 512]) for i in range(2)]
        att_s = [at(f"att_s{i}", 91 + 2 * i, [P, 512]) for i in range(3)]
        att_t = [at(f"att_t{i}", 97 + 2 * i, [P, 4, P]) for i in range(2)]
        vn = at("vn", 115, [P, TT, 512])
        yb = at("yb", 72, [P, TT, 512])
        cp_at = ((101, 103.25, 105.5, 131.5), (57, 59.25, 61.5, 63.75), (45.5, 54, 112, 114.5))
        cp = [[[at(f"cp{b}{d}{r}", cp_at[b][2 * d + r], [P, 4, STEPS + 1, CH]) for r in range(2)] for d in range(2)]
              for b in range(3)]
        sp = [at(f"sp{b}", (66, 48)[b], [P, 2, 2, 4, NCH]) for b in range(2)]
        kf = at("kf", 84, [CH, 8, 15 * CH])
        tm = [at(f"tm{b}", 91.5 + 4 * b, [P, 8, P]) for b in range(2)]
        yn = at("yn", 108, [NCH, STEPS, P])
        ctmp = [at(f"ctmp{i}", 127 + 2.25 * i, [P, 4, STEPS + 1, CH]) for i in range(2)]
        ya = at("ya", 117, [P, 4, TOK])
        mixb_hi = at("mixb_hi", 84, [P, 4, TOK], F32R)
        mixb_lo = at("mixb_lo", 96, [P, 4, TOK], F32R)
        ya_hi = at("ya_hi", 12, [P, 4, TOK], F32R)
        ya_lo = at("ya_lo", 24, [P, 4, TOK], F32R)
        sig = [at(f"sig{i}", 36 + 3 * i, [P, TOK]) for i in range(2)]
        mixa_hi = at("mixa_hi", 48, [P, 4, TOK], F32R)
        mixa_lo = at("mixa_lo", 60, [P, 4, TOK], F32R)
        hid_hi = at("hid_hi", 48, [P, FH, TOK], F32R)
        hid_lo = at("hid_lo", 81, [P, FH, TOK], F32R)
        gpad = at("gpad", 114, [P, PADDED])
        conv = at("conv", 117.25, [P, PADDED])
        hidf = at("hidf", 120.5, [P, TOK])
        z1 = at("z1", 48, [P, 16, TOK])
        fv = at("fv", 0, [P, TT, 4, 256])
        dft = at("dft", 24, [P, 2, 4, 512])
        dftp = at("dftp", 40, [P, 2, 2, 256])
        cs = at("cs", 96, [P, 256])
        prod = at("prod", 124, [P, PADDED])
        pconv = at("pconv", 127.25, [P, PADDED])
        yd = at("yd", 130.5, [P, TOK])
        mixd_hi = at("mixd_hi", 100, [P, 4, TOK], F32R)
        mixd_lo = at("mixd_lo", 112, [P, 4, TOK], F32R)
        mixc_hi = at("mixc_hi", 48, [P, 4, TOK], F32R)
        mixc_lo = at("mixc_lo", 60, [P, 4, TOK], F32R)
        orow = [at(f"orow{i}", 4 * i, [P, D]) for i in range(TT)]
        XB = 2 * 2 * 2 * PAIRS
        ada_acc = (ada_acc0, [bb[0][r][:, :, :].rearrange("p k c -> p (k c)") for r in range(2)])
        ada_row = (ada_row0[:, :], bb[1][0][0:2, :, :].rearrange("p k c -> p (k c)"))

        pj = [ctx.enter_context(nc.psum_tensor(f"pj{u}", [P, 1024], F32)) for u in range(2)]
        pn = ctx.enter_context(nc.psum_tensor("pn", [P, 1024], F32))
        pa = ctx.enter_context(nc.psum_tensor("pa", [P, 512], F32))
        pb = ctx.enter_context(nc.psum_tensor("pb", [P, 512], F32))
        wide = slice(P, P + TOK)
        bank = [pj[0][:, 0:512], pj[0][:, 512:1024], pj[1][:, 0:512], pj[1][:, 512:1024]]

        kbank = ((pn[:, 0:512], pn[:, 512:1024]), (pa[:, :], pb[:, :]))

        const_in = sem("const_in"); x_in = sem("x_in"); rows_in = sem("rows_in"); s5_in = sem("s5_in")
        ada_a_in = [sem(f"ada_a_in{s}") for s in range(3)]; ada_in = [sem(f"ada_in{s}") for s in range(2)]
        c_in = sem("c_in"); c_tr = sem("c_tr"); rows_done = sem("rows_done"); row_ev = sem("row_ev"); row_tr = sem("row_tr")
        ada_v = sem("ada_v"); ada_red = sem("ada_red"); ada_row_ready = sem("ada_row_ready"); ada_tr = sem("ada_tr")
        n_bc = sem("n_bc"); ut_tr = sem("ut_tr"); ut_ev = sem("ut_ev"); spread_in = sem("spread_in")
        q_rt = sem("q_rt"); q_re = sem("q_re"); q_bc = sem("q_bc"); s5g = sem("s5g"); s5r = sem("s5r"); pick0 = sem("pick0")
        mask_in = sem("mask_in"); dft_in = sem("dft_in"); cs_in = sem("cs_in"); ada_b_in = [sem(f"ada_b_in{s}") for s in range(2)]; t_in = sem("t_in"); out_done = sem("out_done")
        raw_in = [sem(f"raw_in{u}") for u in range(2)]
        w_hi_ready = sem("w_hi_ready"); w_lo_ready = sem("w_lo_ready"); job_done = sem("job_done")
        evac = [sem(f"evac{u}") for u in range(2)]
        v_seq = sem("v_seq"); a_seq = sem("a_seq"); g_seq = sem("g_seq")
        fill = sem("fill"); xt_ps = sem("xt_ps"); xt_ev = sem("xt_ev"); vec_ps = sem("vec_ps"); vec_ev = sem("vec_ev")
        c_ps = sem("c_ps"); expanded = sem("expanded"); cond_ready = sem("cond_ready"); ada_done = sem("ada_done")
        mod_ready = sem("mod_ready")
        s5a = sem("s5a"); s5b = sem("s5b"); s5d = sem("s5d")
        n_sq = sem("n_sq"); n_add = sem("n_add"); n_mm = sem("n_mm"); n_sd = sem("n_sd"); n_rs = sem("n_rs"); n_t = sem("n_t")
        n_hf = sem("n_hf"); n_hi = sem("n_hi"); h_ready = sem("h_ready")
        q_sq = sem("q_sq"); q_mm = sem("q_mm"); q_sd = sem("q_sd"); q_rc = sem("q_rc"); q_ready = sem("q_ready")
        v_tr = sem("v_tr"); v_ready = sem("v_ready")
        bias_half = sem("bias_half"); bias_ready = sem("bias_ready")
        a_s = sem("a_s"); a_m = sem("a_m"); a_nm = sem("a_nm"); a_p = sem("a_p"); a_t = sem("a_t")
        a_pt = sem("a_pt"); a_o = sem("a_o"); a_rl = sem("a_rl"); a_y = sem("a_y")
        yb_tr = sem("yb_tr"); yb_hi = sem("yb_hi"); yb_lo = sem("yb_lo")
        u_tr = sem("u_tr"); u_ev = sem("u_ev"); rs_f = sem("rs_f"); rs_b = sem("rs_b"); rt_tr = sem("rt_tr"); rt_ev = sem("rt_ev")
        r_mm = sem("r_mm"); r_ev = sem("r_ev"); x_zero = sem("x_zero")
        sc_mul = sem("sc_mul"); sc_add = sem("sc_add")
        cp_f = sem("cp_f"); cp_b = sem("cp_b"); k_mm = sem("k_mm"); k_ev = sem("k_ev"); sp_ready = sem("sp_ready")
        o_mm = sem("o_mm"); o_ev = sem("o_ev"); y_tr = sem("y_tr"); y_ev = sem("y_ev"); ya_h = sem("ya_h"); ya_l = sem("ya_l")
        glu_s = sem("glu_s"); glu_m = sem("glu_m"); glu_h = sem("glu_h"); glu_l = sem("glu_l")
        cv = sem("cv"); sl = sem("sl"); hh = sem("hh"); hl = sem("hl"); pad_zero = sem("pad_zero")
        gate0 = sem("gate0"); up0 = sem("up0")
        f_mm = sem("f_mm"); f_ev = sem("f_ev"); fy_mm = sem("fy_mm"); fy_hi = sem("fy_hi"); fy_lo = sem("fy_lo")
        d_seq = sem("d_seq"); d_f = sem("d_f"); d_h = sem("d_h"); d_l = sem("d_l")
        out_tr = sem("out_tr"); out_ev = sem("out_ev")

        block = ctx.enter_context(nc.Block())

        def wait_pos(eng, s, v):
            if not isinstance(v, int) or v > 0:
                eng.wait_ge(s, v)

        def pairs(eng, count, body, peel=1):
            for i in range(peel):
                body(i)
            if count // 2 > peel + 1:
                with eng.Fori(peel, count // 2 - 1) as i:
                    body(i)
            body(count // 2 - 1)

        def ahead(first, i, u, own):
            return depth(first + 2 * i + u + 2) if isinstance(i, int) else own

        STAGES = []
        w_in = (t["ab_w_in"][0], t["cd_w_in"][0])
        w_out = (t["ab_w_out"][0], t["cd_w_out"][0])
        for layer in range(2):
            w = w_in[layer].rearrange("(k p) (j c) -> j p k c", p=P, c=P)
            if layer == 0:
                STAGES.append((J_IN[0], 16, w, None))
            else:
                STAGES.append((J_IN[1], 12, w[4:16], None))
                STAGES.append((J_IN[1] + 12, 4, w[0:4], None))
            if layer == 0:
                STAGES.append((J_GLU, 4, t["s5_w_glu"][0].rearrange("(k p) (j c) -> j p k c", p=P, c=P), None))
            STAGES.append((J_OUT[layer], KD, w_out[layer].rearrange("(k p) (j c) -> j p k c", p=P, c=P), None))
            for half in range(2):
                gate = t["ffn_w_gate"][layer].rearrange("(k p) (j c) -> j p k c", p=P, c=P)[half * FH:(half + 1) * FH]
                up = t["ffn_w_up"][layer].rearrange("(k p) (j c) -> j p k c", p=P, c=P)[half * FH:(half + 1) * FH]
                STAGES.append((J_UP[layer][half], 2 * FH, gate, up))
                down = t["ffn_w_down"][layer].rearrange("(h k p) (j c) -> h j p k c", h=2, p=P, c=P)[half]
                STAGES.append((J_DOWN[layer][half], KD, down, None))

        ada_src = t["ada_w"].rearrange("l (h k p) (j c) -> h l j p k c", h=2, p=P, c=ADA)

        @block.sync
        def _(sp_e):
            sp_e.dma_start(ident[:, :], t["c_ident"]).then_inc(const_in, 16)
            sp_e.dma_start(blk[:, :], t["c_blk"]).then_inc(const_in, 16)
            for r in range(2):
                src = (t["x_prompt"], t["x_sample"])[r][0]
                sp_e.dma_start(xrows[:, START[r] // P:(START[r] + SEQ[r]) // P, :],
                               src.rearrange("(n p) d -> p n d", p=P)).then_inc(x_in, 16)
            for k in range(4):
                if k == 3:
                    sp_e.wait_ge(rows_done, 1)
                sp_e.dma_start(ada_a[k % 3][:, :, :],
                               t["ada_w"][0].rearrange("(k p) (j c) -> j p k c", p=P, c=512)[k]).then_inc(ada_a_in[k % 3], 16)
            def ada_load(e):
                for h in range(2):
                    wait_pos(sp_e, ada_v, 16 * (e - 1) + 8 * (h + 1))
                    sp_e.dma_start(ada_w[h][:, :, :], ada_src[h][0][8 + e]).then_inc(ada_in[h], 16)

            for first, count, src, src2 in STAGES:
                def body(i, first=first, src=src, src2=src2):
                    for u in range(2):
                        wait_pos(sp_e, w_lo_ready, first + 2 * i + u - 1)
                        w = src2[i] if (src2 is not None and u) else src[i] if src2 is not None else src[2 * i + u]
                        sp_e.dma_start(w_raw[u][:, 0:depth(first), :], w).then_inc(raw_in[u], 16)
                        if first == J_IN[0] and not (isinstance(i, int) and i == 0):
                            ada_load(2 * i + u - 2)
                if first == J_IN[0]:
                    body(0)
                    body(1)
                    with sp_e.Fori(2, count // 2 - 1) as i:
                        body(i)
                    body(count // 2 - 1)
                    ada_load(14)
                elif first == J_GLU:
                    body(0)
                    ada_load(15)
                    sp_e.wait_ge(ada_v, 16 * 16)
                    sp_e.dma_start(spread[:, :, :], t["c_spread"]).then_inc(spread_in, 16)
                    sp_e.wait_ge(q_ready, 8)
                    sp_e.dma_start(dist[:, :], t["c_dist"]).then_inc(mask_in, 16)
                    sp_e.dma_start(lnc[:, :], t["c_lnc"]).then_inc(mask_in, 16)
                    body(1)
                elif first == J_OUT[1]:
                    body(0)
                    sp_e.wait_ge(job_done, J_IN[1] + 16)
                    for s in range(2):
                        sp_e.dma_start(dft[:, s, :, :], t["c_dft"][s].rearrange("(k p) n -> p k n", p=P)).then_inc(dft_in, 16)
                        sp_e.dma_start(dftp[:, s, :, :], t["c_dftp"][s].rearrange("(k p) n -> p k n", p=P)).then_inc(dft_in, 16)
                    with sp_e.Fori(1, count // 2 - 1) as i:
                        body(i)
                    body(count // 2 - 1)
                else:
                    if first == J_IN[1] + 12:
                        sp_e.wait_ge(job_done, J_IN[1])
                        sp_e.dma_start(cs[:, :], t["c_cs"]).then_inc(cs_in, 16)
                    pairs(sp_e, count, body)
                if first == J_GLU:
                    for q in range(4):
                        sp_e.wait_ge(k_ev, 4 * q + 4)
                        wait_pos(sp_e, o_mm, 2 * (q - 1))
                        for j in range(STEPS):
                            sp_e.dma_start(tm[q % 2][CH * j:CH * j + CH, :, :],
                                           kf[:, :, (STEPS - 1 - j) * CH:(STEPS - 1 - j) * CH + P]).then_inc(t_in, 16)
            for n in range(TT):
                sp_e.wait_ge(out_ev, 2 * n + 2)
                dst = y_prompt[0] if n < 2 else y_sample[0]
                row = n * P if n < 2 else (n - 2) * P
                sp_e.dma_start(dst[row:row + P, :], orow[n][:, :]).then_inc(out_done, 16)
            sp_e.wait_ge(out_done, 16 * TT)

        @block.gpsimd
        def _(g):
            count = [0]

            def link(ins):
                count[0] += 1
                ins.then_inc(g_seq, 1)
                g.wait_ge(g_seq, count[0])

            def tt(o, x, y, op):
                link(nc.gpsimd.tensor_tensor(o, x, y, op))

            def ts(o, x, c0, c1=None, op0=ALU.mult, op1=ALU.add):
                link(nc.gpsimd.tensor_scalar(o, x, c0, c1, op0, op1) if c1 is not None else nc.gpsimd.tensor_scalar(o, x, c0, None, op0))

            nc.gpsimd.memset(ones[:, :], 1.0).then_inc(fill, 1)
            nc.gpsimd.memset(eps[:, :], EPS).then_inc(fill, 1)
            nc.gpsimd.memset(pick[:, :, :], 0.0).then_inc(pick0, 1)
            g.wait_ge(pick0, 1)
            nc.gpsimd.memset(pick[:, 0, 0:1], 1.0).then_inc(fill, 1)
            nc.gpsimd.memset(pick[:, 1, 1:2], 1.0).then_inc(fill, 1)

            def norm(k):
                for j in range(KD):
                    g.wait_ge(n_hi, KD * k + j + 1)
                    nc.gpsimd.tensor_tensor(h_lo[:, j, :], hf[j % 2][:, :], h_hi[:, j, :].bitcast(F32), ALU.subtract).then_inc(h_ready, 1)

            def accumulate(k):
                for j in range(KD):
                    g.wait_ge(n_sq, KD * k + j + 1)
                    if j == 0:
                        nc.gpsimd.tensor_copy(sq_acc[:, :], sq_later[0][:, :]).then_inc(n_add, 1)
                    else:
                        g.wait_ge(n_add, KD * (k - 1) + j)
                        nc.gpsimd.tensor_tensor(sq_acc[:, :], sq_acc[:, :], sq_later[j % 2][:, :], ALU.add).then_inc(n_add, 1)
            norm(0)
            g.wait_ge(vec_ev, 5)
            ts(ct[2][:, :, :], ct[0][:, :, :], -1.0)
            RE, IM, DT, MAG, TH, R, SIN, SH = (s5v[:, i, :] for i in (1, 2, 3, 5, 6, 8, 9, 10))
            T1, T2, T3, AR, AI, AM, CR, CI = (s5v[:, i, :] for i in (11, 12, 13, 14, 15, 16, 17, 18))
            g.wait_ge(s5a, 1)
            nc.gpsimd.tensor_tensor(s5v[:, 4, :], RE, DT, ALU.mult).then_inc(s5d, 1)
            tt(TH, IM, DT, ALU.mult)
            ts(T1, TH, 1.0 / (2 * math.pi), MAGIC)
            ts(T2, T1, -MAGIC, op0=ALU.add)
            for part in (TWO_PI_HI, TWO_PI_MID, TWO_PI_LO):
                ts(T3, T2, -part)
                tt(TH, TH, T3, ALU.add)
            nc.gpsimd.tensor_scalar(R, TH, 3.1415925, -3.1415925, ALU.min, ALU.max).then_inc(s5d, 1)
            tt(T1, RE, RE, ALU.mult)
            tt(T2, IM, IM, ALU.mult)
            nc.gpsimd.tensor_tensor(T3, T1, T2, ALU.add).then_inc(s5g, 1)
            g.wait_ge(s5a, 4)
            g.wait_ge(s5g, 1)
            tt(T1, SH, SH, ALU.mult)
            ts(T2, T1, -2.0, 1.0)
            tt(AR, MAG, T2, ALU.mult)
            tt(AI, MAG, SIN, ALU.mult)
            ts(AM, AR, -1.0, op0=ALU.add)
            g.wait_ge(s5r, 1)
            tt(T1, AM, RE, ALU.mult)
            tt(T2, AI, IM, ALU.mult)
            tt(T1, T1, T2, ALU.add)
            tt(CR, T1, T3, ALU.mult)
            tt(T1, AI, RE, ALU.mult)
            tt(T2, AM, IM, ALU.mult)
            tt(T1, T1, T2, ALU.subtract)
            tt(CI, T1, T3, ALU.mult)
            for d in range(2):
                cr, ci = (x[:, PAIRS * d:PAIRS * d + PAIRS].unsqueeze(2).broadcast_to([P, PAIRS, CH]) for x in (CR, CI))
                x1, x2 = s5t[0][:, :, :], s5t[1][:, :, :]
                tt(x1, braw[0][:, :, :], cr, ALU.mult)
                tt(x2, braw[1][:, :, :], ci, ALU.mult)
                tt(bb[d][0][:, :, :], x1, x2, ALU.subtract)
                tt(x1, braw[1][:, :, :], cr, ALU.mult)
                tt(x2, braw[0][:, :, :], ci, ALU.mult)
                tt(bb[d][1][:, :, :], x1, x2, ALU.add)
            ar, ai = (x.rearrange("p (d k) -> p d k", d=2) for x in (AR, AI))
            t1, t2 = (x.rearrange("p (d k) -> p d k", d=2) for x in (T1, T2))
            link(nc.gpsimd.memset(powr[0][:, :, :, 0], 1.0))
            link(nc.gpsimd.memset(powr[1][:, :, :, 0], 0.0))
            for e in range(1, STEPS + 1):
                pr, pi = powr[0][:, :, :, e - 1], powr[1][:, :, :, e - 1]
                tt(t1, pr, ar, ALU.mult)
                tt(t2, pi, ai, ALU.mult)
                tt(powr[0][:, :, :, e], t1, t2, ALU.subtract)
                tt(t1, pr, ai, ALU.mult)
                tt(t2, pi, ar, ALU.mult)
                tt(powr[1][:, :, :, e], t1, t2, ALU.add)
            for r in range(2):
                for ri in range(2):
                    link(nc.gpsimd.tensor_copy(stepA[:, ri, :, r, :], powr[0][:, :, :, STEPS]))
                ts(stepB[:, 1, :, r, :], powr[1][:, :, :, STEPS], -1.0)
                last = nc.gpsimd.tensor_copy(stepB[:, 0, :, r, :], powr[1][:, :, :, STEPS])
                if r == 0:
                    link(last)
            last.then_inc(s5g, 1)
            g.wait_ge(job_done, J_IN[0] + 16)
            nc.gpsimd.memset(xs[:, :, :, :, :, :], 0.0).then_inc(x_zero, 1)
            g.wait_ge(q_ready, 8)
            for q in range(4):
                wait_pos(g, rt_tr, 4 * q)
                ks = slice(4 * q, 4 * q + 4)
                pr, pi = (powr[r][:, 1, ks, 0:STEPS].unsqueeze(3).broadcast_to([P, 4, STEPS, CH]) for r in range(2))
                br, bi = (bb[1][r][:, ks, :].unsqueeze(2).broadcast_to([P, 4, STEPS, CH]) for r in range(2))
                t1, t2 = (rtmp[1][i][:, :, :, :] for i in range(2))
                tt(t1, pr, br, ALU.mult)
                tt(t2, pi, bi, ALU.mult)
                tt(rs[1][0][:, :, :, :], t1, t2, ALU.subtract)
                tt(t1, pr, bi, ALU.mult)
                tt(t2, pi, br, ALU.mult)
                nc.gpsimd.tensor_tensor(rs[1][1][:, :, :, :], t1, t2, ALU.add).then_inc(rs_b, 1)
                g.wait_ge(rs_b, q + 1)
            g.wait_ge(r_ev, 64)
            def flat(ap):
                return ap.rearrange("p r d q k -> p r (d q k)")
            for m in range(1, MCH):
                prev = xs[:, m, :, :, :, :].rearrange("p r d q k -> p r (d q k)")
                new = xs[:, m + 1, :, :, :, :].rearrange("p r d q k -> p r (d q k)")
                s0, s1 = (scan[i][:, :].rearrange("p (r k) -> p r k", r=2) for i in range(2))
                nc.gpsimd.tensor_tensor(s0, prev, flat(stepA[:, :, :, :, :]), ALU.mult).then_inc(sc_mul, 1)
                nc.gpsimd.tensor_tensor(s1, prev, flat(stepB[:, :, :, :, :]), ALU.mult).then_inc(sc_mul, 1)
                g.wait_ge(sc_mul, 2 * m)
                nc.gpsimd.tensor_tensor(new, new, s0, ALU.add).then_inc(sc_add, 1)
                g.wait_ge(sc_add, 2 * m - 1)
                nc.gpsimd.tensor_tensor(new, new, s1[:, ::-1, :], ALU.add).then_inc(sc_add, 1)
                g.wait_ge(sc_add, 2 * m)
            for layer in range(2):
                if layer:
                    accumulate(2)
                    norm(2)
                    for c in (0, SEQ[0] + 1, PADDED - 1):
                        nc.gpsimd.memset(prod[:, c:c + 1], 0.0).then_inc(pad_zero, 1)
                accumulate(2 * layer + 1)
                norm(2 * layer + 1)
                for c in (0, SEQ[0] + 1, PADDED - 1):
                    nc.gpsimd.memset(gpad[:, c:c + 1], 0.0).then_inc(pad_zero, 1)
                if layer == 0:
                    for e in range(16, 40):
                        for h in range(2):
                            g.wait_ge(ada_v, 16 * (e - 1) + 8 * (h + 1))
                            g.dma_start(ada_w[h][:, :, :], ada_src[h][1][e - 16]).then_inc(ada_b_in[h], 16)

        @block.scalar
        def _(a):
            for r, name in enumerate(("c_prompt", "c_sample")):
                a.dma_start(crows[KD * r:KD * (r + 1), :], t[name][0].rearrange("(k p) -> k p", p=P)).then_inc(c_in, 16)
            rows = [
                (rowsA[0:16, :], t["norm_mix_g"].rearrange("l (k p) -> (l k) p", p=P)),
                (rowsA[16:32, :], t["norm_ffn_g"].rearrange("l (k p) -> (l k) p", p=P)),
                (rowsA[32:128, :], t["ada_b"].rearrange("l (k p) -> (l k) p", p=P)),
                (rowsB[0:66, :], t["ffn_conv_w"][0].rearrange("w (k p) -> (w k) p", p=P)),
                (rowsB[66:88, :], t["ffn_conv_b"][0].rearrange("(k p) -> k p", p=P)),
                (rowsB[88:92, :], t["s5_b_glu"][0].rearrange("(k p) -> k p", p=P)),
                (rowsB[92:104, :], t["sconv_w"][0].rearrange("w (k p) -> (w k) p", p=P)),
                (rowsB[QG:QG + 1, 0:64], t["q_norm_g"]), (rowsB[QG:QG + 1, 64:128], t["q_norm_g"]),
                (rowsB[QG + 1:QG + 2, 0:64], t["k_norm_g"]), (rowsB[QG + 1:QG + 2, 64:128], t["k_norm_g"]),
                (rowsC[0:66, :], t["ffn_conv_w"][1].rearrange("w (k p) -> (w k) p", p=P)),
                (rowsC[66:88, :], t["ffn_conv_b"][1].rearrange("(k p) -> k p", p=P)),
                (rowsS[32:48, :], t["s5_lam_re_f"][0].rearrange("(k h) p -> k (h p)", h=2)),
                (rowsS[48:64, :], t["s5_lam_re_b"][0].rearrange("(k h) p -> k (h p)", h=2)),
                (rowsS[64:80, :], t["s5_lam_im_f"][0].rearrange("(k h) p -> k (h p)", h=2)),
                (rowsS[80:96, :], t["s5_lam_im_b"][0].rearrange("(k h) p -> k (h p)", h=2)),
                (ldt[0:16, :], t["s5_log_dt_f"][0].rearrange("(k h) -> k h", h=2)),
                (ldt[16:32, :], t["s5_log_dt_b"][0].rearrange("(k h) -> k h", h=2)),
            ]
            assert len(rows) == ROW_DMAS
            for dst, src in rows:
                a.dma_start(dst, src).then_inc(rows_in, 16)
            for r, (b, c) in enumerate((("s5_b_re", "s5_c_re"), ("s5_b_im", "s5_c_im"))):
                for h in range(2):
                    a.dma_start(braw[r][64 * h:64 * h + 64, :, :],
                                t[b][0].rearrange("(k h) p c -> h p k c", h=2)[h]).then_inc(s5_in, 16)
                    a.dma_start(crow[r][:, :, h, :],
                                t[c][0].rearrange("(k g) c p -> (g c) k p", g=8)).then_inc(s5_in, 16)
            a.dma_start(drow[:, :, :], t["s5_d"].rearrange("o (g c) -> o g c", c=CH).broadcast_to([CH, GRP, CH])
                        ).then_inc(s5_in, 16)

            def next_split(first, i, u, own):
                n = first + 2 * i + u
                if isinstance(i, int) and n + 2 >= JOBS:
                    a.wait_ge(job_done, n + 1)
                    return
                k = ahead(first, i, u, own)
                a.wait_ge(job_done, n + 1)
                a.wait_ge(raw_in[u], 16 * (first // 2 + i + 2))
                nc.scalar.activation(w_hi[u][:, 0:k, :], w_raw[u][:, 0:k, :], ACT.Copy).then_inc(w_hi_ready, 1)

            def row_copy(layer, e):
                a.wait_ge(ada_red, e + 1)
                wait_pos(a, ada_tr, e)
                nc.scalar.activation(ada_row[layer], pa[0:2, 0:ADA], ACT.Copy).then_inc(ada_row_ready, 1)

            def square(k, j, sq):
                wait_pos(a, n_add if k else n_mm, KD * max(k - 1, 0) + j - 1)
                nc.scalar.activation(sq[:, :], xT[:, j, :], ACT.Square).then_inc(n_sq, 1)

            def norm(k):
                a.wait_ge(n_mm, KD + k)
                nc.scalar.activation(rms[:, :], pn[:, 0:TT], ACT.Sqrt, bias=eps[:, 0:1], scale=1.0 / D).then_inc(n_sd, 1)
                for j in range(KD):
                    m = KD * k + j
                    a.wait_ge(n_hf, 2 * m + 2)
                    nc.scalar.activation(h_hi[:, j, :], hf[j % 2][:, :], ACT.Copy).then_inc(n_hi, 1)

            a.wait_ge(fill, 4)
            a.wait_ge(c_tr, 1)
            nc.scalar.activation(cond[:, :, :], pa[:, 0:2 * KD].rearrange("p (r k) -> p k r", r=2), ACT.Silu).then_inc(cond_ready, 1)
            a.wait_ge(xt_ev, 12)
            for k in range(4):
                for j in (2 * k, 2 * k + 1):
                    square(0, j, sq_first[j % 2])
                a.wait_ge(rows_done, k + 1)
                wait_pos(a, row_tr, k - 1)
                nc.scalar.activation(mod_row[k % 2][:, :], (pa, pb)[k % 2][0:2, :], ACT.Copy).then_inc(row_ev, 1)
            a.wait_ge(vec_ev, 4)
            nc.scalar.activation(s5v[:, 3, :], s5v[:, 0, :], ACT.Exp).then_inc(s5a, 1)
            a.wait_ge(raw_in[0], 16)
            nc.scalar.activation(w_hi[0][:, 0:KD, :], w_raw[0][:, 0:KD, :], ACT.Copy).then_inc(w_hi_ready, 1)
            a.wait_ge(raw_in[1], 16)
            nc.scalar.activation(w_hi[1][:, 0:KD, :], w_raw[1][:, 0:KD, :], ACT.Copy).then_inc(w_hi_ready, 1)
            norm(0)

            def out_stage(first, own, count, k=None, after=None):
                def body(i):
                    for u in range(2):
                        next_split(first, i, u, own)
                        if k is not None:
                            a.wait_ge(evac[u], first // 2 + i + 1)
                            square(k, 2 * i + u, sq_later[u])
                        if after is not None:
                            after(i, u)
                pairs(a, count, body)

            def ffn(layer):
                for half in range(2):
                    first = J_UP[layer][half]
                    seen = (2 * layer + half) * FH
                    a.wait_ge(pad_zero, 6 * layer + 3)

                    def body(i, first=first, seen=seen):
                        next_split(first, i, 0, KD)
                        wait_pos(a, cv, 3 * (seen + i))
                        nc.scalar.activation(gpad[:, 1:1 + SEQ[0]], pj[0][:, P:P + SEQ[0]], ACT.Copy).then_inc(gate0, 1)
                        nc.scalar.activation(gpad[:, 2 + SEQ[0]:2 + TOK], pj[0][:, P + SEQ[0]:P + TOK], ACT.Copy).then_inc(evac[0], 1)
                        next_split(first, i, 1, KD)
                        a.wait_ge(cv, 3 * (seen + i) + 3)
                        nc.scalar.activation(conv[:, 0:TOK + 1], conv[:, 0:TOK + 1], ACT.Silu).then_inc(sl, 1)
                        a.wait_ge(evac[1], first // 2 + i + 1)
                        nc.scalar.activation(hid_hi[:, i, :], hidf[:, :], ACT.Copy).then_inc(hh, 1)
                        if layer == 0 and not (half == 0 and isinstance(i, int) and i == 0):
                            row_copy(1, (15, 28)[half] + i)
                    pairs(a, 2 * FH, body)

                    def after(i, u, half=half):
                        if u == 1 and isinstance(i, int):
                            if half == 0:
                                row_copy(1, 26 if i == 0 else 27)
                            elif i == 0:
                                row_copy(1, 39)
                    if layer == 0 and half == 1:
                        a.wait_ge(ada_v, 16 * 40)
                    out_stage(J_DOWN[layer][half], FH, KD, 2 if layer == 0 and half == 1 else None, after if layer == 0 else None)

            def in_body(i):
                for u in range(2):
                    n = 2 * i + u
                    next_split(0, i, u, KD)
                    fixed = isinstance(n, int)
                    if fixed and n < 4:
                        wait_pos(a, ut_tr, n - 1)
                        nc.scalar.activation(ut[u][:, :], pj[u][:, wide], ACT.Copy).then_inc(evac[u], 1)
                    else:
                        nc.scalar.activation(z0[:, n - 4, :], pj[u][:, wide], ACT.Copy).then_inc(evac[u], 1)
                    if fixed and 1 <= n <= 4:
                        a.wait_ge(ut_tr, n)
                        for b in range(2):
                            src = pn[0:NCH, 512 * b:512 * b + 512].rearrange("n (j g c) -> n j g c", g=8, c=CH)
                            dst = un[:, 8 * (n - 1):8 * n, 4 * b:4 * b + 4, :].rearrange("n g j c -> n j g c")
                            nc.scalar.activation(dst, src, ACT.Copy).then_inc(ut_ev, 1)
                    row_copy(0, n)
                    if fixed and n == 0:
                        a.wait_ge(s5d, 1)
                        nc.scalar.activation(s5v[:, 5, :], s5v[:, 4, :], ACT.Exp).then_inc(s5a, 1)
                    if fixed and n == 1:
                        a.wait_ge(s5d, 2)
                        nc.scalar.activation(s5v[:, 9, :], s5v[:, 8, :], ACT.Sin).then_inc(s5a, 1)
                        nc.scalar.activation(s5v[:, 10, :], s5v[:, 8, :], ACT.Sin, scale=0.5).then_inc(s5a, 1)
            for i in range(3):
                in_body(i)
            with a.Fori(3, 7) as i:
                in_body(i)
            in_body(7)
            for u in range(2):
                a.wait_ge(evac[u], 8)
            a.wait_ge(s5g, 2)
            for k in range(8):
                wait_pos(a, q_mm, k - 1)
                nc.scalar.activation(qsq[k % 2][:, :], z0[:, k, :], ACT.Square).then_inc(q_sq, 1)
            a.wait_ge(q_mm, 8)
            nc.scalar.activation(qrms[:, :, :].rearrange("p b h -> p (b h)"), pn[:, 0:TT * 2 * HEADS], ACT.Sqrt, bias=eps[:, 0:1],
                                 scale=1.0 / HD).then_inc(q_sd, 1)
            a.wait_ge(q_rt, 1)
            nc.scalar.activation(q_rows[:, :], pj[0][0:2 * HEADS, wide], ACT.Copy).then_inc(q_re, 1)
            def chunks(q):
                for b in range(2):
                    a.wait_ge(u_tr, 2 * q + b + 1)
                    nc.scalar.activation(uc[:, 8 * q + 4 * b:8 * q + 4 * b + 4, :],
                                         (pa, pb)[b][:, 0:4 * NCH].rearrange("p (g n) -> p g n", n=NCH), ACT.Copy).then_inc(u_ev, 1)
            chunks(0)
            for q in range(4):
                wait_pos(a, r_mm, 4 * q)
                for b in range(4):
                    a.wait_ge(rt_tr, 4 * q + b + 1)
                    nc.scalar.activation(rt[:, :, :, b // 2, b % 2, :],
                                         bank[b][:, :].rearrange("p (k h s) -> p k h s", h=2, s=64), ACT.Copy).then_inc(rt_ev, 1)
                if q < 3:
                    chunks(q + 1)

            def expo(n):
                a.wait_ge(a_nm, n + 1)
                w = SEQ[0] if n % TT < 2 else SEQ[1]
                nc.scalar.activation(att_s[n % 3][:, 0:w], att_s[n % 3][:, 0:w], ACT.Exp, bias=att_nm[:, n:n + 1],
                                     accum_out=att_l[:, n:n + 1]).then_inc(a_p, 1)
            expo(0)
            for n in range(48):
                if n < 47:
                    expo(n + 1)
                nk = (2 if n % TT < 2 else 4)
                a.wait_ge(a_t, n + 1)
                wait_pos(a, a_o, n - 1)
                nc.scalar.activation(att_t[n % 2][:, 0:nk, :], (pa, pb)[n % 2][:, 0:nk * P].rearrange("p (k q) -> p k q", q=P), ACT.Copy).then_inc(a_pt, 1)

            def states(q):
                for b in range(2):
                    a.wait_ge(k_mm, 2 * q + b + 1)
                    wait_pos(a, t_in, 128 * q)
                    for h in range(2):
                        nc.scalar.activation(kf[:, 4 * b + h:4 * b + 4:2, :],
                                             kbank[b][h][0:CH, :].rearrange("p (g n) -> p g n", g=2)[:, :, 0:15 * CH],
                                             ACT.Copy).then_inc(k_ev, 1)
                if q == 0:
                    a.wait_ge(sc_add, 2 * (MCH - 1))
                wait_pos(a, o_mm, 2 * (q - 1))
                ks = slice(4 * q, 4 * q + 4)
                for r in range(2):
                    m = CHUNKS[r]
                    c0 = START[r] // STEPS
                    for ri in range(2):
                        nc.scalar.activation(sp[q % 2][:, 0, ri, :, c0:c0 + m], xs[:, 0:m, ri, 0, r, ks].rearrange("p m k -> p k m"),
                                             ACT.Copy).then_inc(sp_ready, 1)
                        nc.scalar.activation(sp[q % 2][:, 1, ri, :, c0:c0 + m],
                                             xs[:, 0:m, ri, 1, r, ks][:, ::-1, :].rearrange("p m k -> p k m"),
                                             ACT.Copy).then_inc(sp_ready, 1)
            states(0)
            for q in range(4):
                if q < 3:
                    states(q + 1)
                for b in range(2):
                    a.wait_ge(o_mm, 2 * q + b + 1)
                    wait_pos(a, y_tr, 2 * q)
                    nc.scalar.activation(yn[:, :, :].rearrange("n i (g h c) -> n h g i c", h=2, c=CH)[:, b],
                                         bank[b][0:NCH, :].rearrange("n (g i c) -> n g i c", i=STEPS, c=CH),
                                         ACT.Gelu_apprx_tanh).then_inc(o_ev, 1)
            for k in range(4):
                a.wait_ge(y_ev, 2 * k + 2)
                nc.scalar.activation(ya_hi[:, k, :], ya[:, k, :], ACT.Copy).then_inc(ya_h, 1)
                a.wait_ge(yb_tr, k + 1)
                nc.scalar.activation(mixb_hi[:, k, :], pj[k % 2][:, wide], ACT.Copy).then_inc(yb_hi, 1)
            for k in range(4):
                u = k % 2
                next_split(J_GLU, k // 2, u, 4)
                wait_pos(a, glu_l, k - 1)
                nc.scalar.activation(sig[u][:, :], pj[u][:, wide], ACT.Sigmoid, bias=vecB[:, 88 + k:89 + k]).then_inc(evac[u], 1)
                a.wait_ge(glu_m, k + 1)
                nc.scalar.activation(mixa_hi[:, k, :], sig[u][:, :], ACT.Copy).then_inc(glu_h, 1)
            out_stage(J_OUT[0], KD, KD, 1)
            norm(1)
            ffn(0)
            norm(2)

            def z1body(i):
                for u in range(2):
                    next_split(J_IN[1], i, u, KD)
                    nc.scalar.activation(z1[:, 2 * i + u, :], pj[u][:, wide], ACT.Copy).then_inc(evac[u], 1)
            pairs(a, 12, z1body)
            for k in range(4):
                next_split(J_IN[1] + 12, k // 2, k % 2, KD)
                nc.scalar.activation(z1[:, 12 + k, :], pj[k % 2][:, wide], ACT.Copy).then_inc(evac[k % 2], 1)
                a.wait_ge(d_f, k + 1)
                nc.scalar.activation(mixd_hi[:, k, :], yd[:, :], ACT.Copy).then_inc(d_h, 1)
            for n in range(2 * TT):
                a.wait_ge(f_mm, n + 1)
                nc.scalar.activation(fv[:, n // 2, 2 * (n % 2):2 * (n % 2) + 2, :],
                                     bank[n % 4].rearrange("p (g c) -> p g c", g=2), ACT.Copy).then_inc(f_ev, 1)
            for k in range(4):
                a.wait_ge(fy_mm, k + 1)
                if k == 0:
                    a.wait_ge(d_l, 4)
                nc.scalar.activation(mixc_hi[:, k, :], pj[k % 2][:, wide], ACT.Copy).then_inc(fy_hi, 1)
            out_stage(J_OUT[1], KD, KD, 3)
            norm(3)
            ffn(1)

        @block.vector
        def _(v):
            count = [0]

            def link(ins):
                count[0] += 1
                ins.then_inc(v_seq, 1)
                v.wait_ge(v_seq, count[0])

            def tt(o, x, y, op):
                link(nc.vector.tensor_tensor(o, x, y, op))

            def low(n, u, k):
                v.wait_ge(w_hi_ready, n + 1)
                nc.vector.tensor_tensor(w_lo[u][:, 0:k, :], w_raw[u][:, 0:k, :], w_hi[u][:, 0:k, :].bitcast(F32),
                                        ALU.subtract).then_inc(w_lo_ready, 1)

            def next_low(first, i, u, own):
                if isinstance(i, int) and first + 2 * i + u + 2 >= JOBS:
                    return
                low(first + 2 * i + u + 2, u, ahead(first, i, u, own))

            def ada_step(layer, e):
                for kt in range(KD):
                    h, k = divmod(kt, KD // 2)
                    if k == 0:
                        v.wait_ge(ada_b_in[h] if layer else ada_in[h], 16 * (e - 15 if layer else e + 1))
                    if kt == 0:
                        wait_pos(v, ada_red, e)
                    for r in range(2):
                        acc = ada_acc[layer][r] if layer else ada_acc0[r][:, :]
                        if kt == 0:
                            ins = nc.vector.tensor_scalar(acc, ada_w[h][:, k, :], cond[:, kt, r:r + 1], None, ALU.mult)
                        else:
                            v.wait_ge(ada_v, 16 * e + 2 * (kt - 1) + r + 1)
                            ins = nc.vector.scalar_tensor_tensor(acc, ada_w[h][:, k, :], cond[:, kt, r:r + 1], acc, ALU.mult, ALU.add)
                        ins.then_inc(ada_v, 1)

            def modulation(layer, lo, hi, src, s5b_count):
                nc.vector.tensor_tensor(mod[:, layer, lo:hi, :], src.rearrange("p (k r) -> p k r", r=2),
                                        vecA[:, 32 + 48 * layer + lo:32 + 48 * layer + hi].unsqueeze(2).broadcast_to([P, hi - lo, 2]),
                                        ALU.add).then_inc(s5b, 1)
                v.wait_ge(s5b, s5b_count)

            def gains(layer, which):
                nc.vector.scalar_tensor_tensor(gain[:, layer, which, :, :], mod[:, layer, 24 * which + 8:24 * which + 16, :], 1.0,
                                               vecA[:, 16 * which + 8 * layer:16 * which + 8 * layer + 8].unsqueeze(2).broadcast_to([P, KD, 2]),
                                               ALU.add, ALU.mult).then_inc(mod_ready, 1)
                v.wait_ge(mod_ready, 2 * layer + which + 1)

            for n in range(12):
                v.wait_ge(xt_ps, n + 1)
                nc.vector.tensor_copy(xT[:, 4 * (n % 2):4 * (n % 2) + 4, P * (n // 2):P * (n // 2) + P],
                                      bank[n % 4].rearrange("p (k c) -> p k c", k=4)).then_inc(xt_ev, 1)
            v.wait_ge(rows_in, 16 * ROW_DMAS)
            nc.vector.tensor_copy(rowsS[0:32, :].rearrange("p (h s) -> p h s", h=2),
                                  ldt[:, :].unsqueeze(2).broadcast_to([32, 2, 64])).then_inc(expanded, 1)
            v.wait_ge(vec_ps, 4)
            nc.vector.tensor_copy(vecA[:, :], bank[1][:, 0:128]).then_inc(vec_ev, 1)
            nc.vector.tensor_copy(vecB[:, 0:QG + 2], bank[1][:, 128:128 + QG + 2]).then_inc(vec_ev, 1)
            nc.vector.tensor_copy(vecC[:, 0:88], bank[1][:, 256:344]).then_inc(vec_ev, 1)
            nc.vector.tensor_copy(s5v[:, 0:3, :], bank[1][:, 384:480].rearrange("p (k c) -> p k c", k=3)).then_inc(vec_ev, 1)
            v.wait_ge(vec_ev, 4)
            link(nc.vector.tensor_scalar(vecB[:, QG:QG + 1], vecB[:, QG:QG + 1], 1.0 / math.sqrt(HD), None, ALU.mult))
            v.wait_ge(s5_in, 16 * 9)
            v.wait_ge(const_in, 32)
            tt(ddiag[:, :, :], drow[:, :, :], ident[0:CH, 0:CH].unsqueeze(1).broadcast_to([CH, GRP, CH]), ALU.mult)
            v.wait_ge(c_ps, 2)
            for r in range(2):
                src = bank[2 + r].rearrange("p (k h c) -> p k h c", h=2, c=CH)
                for h in range(2):
                    ins = nc.vector.tensor_copy(ct[r][64 * h:64 * h + 64, :, :], src[64 * h:64 * h + 64, :, h, :])
                    if r == 1 and h == 1:
                        ins.then_inc(vec_ev, 1)
                    else:
                        link(ins)
            low(0, 0, KD)
            v.wait_ge(row_tr, 4)
            modulation(0, 0, 16, bank[0][:, 0:32], 1)
            gains(0, 0)
            low(1, 1, KD)

            def norm(k):
                layer, which = divmod(k, 2)
                v.wait_ge(n_sd, k + 1)
                nc.vector.reciprocal(rms[:, :], rms[:, :]).then_inc(n_rs, 1)
                v.wait_ge(n_bc, k + 1)
                for j in range(KD):
                    m = KD * k + j
                    wait_pos(v, n_hf, 2 * (m - 1))
                    nc.vector.tensor_tensor(nt[j % 2][:, :], xT[:, j, :], pn[:, wide], ALU.mult).then_inc(n_t, 1)
                    v.wait_ge(n_t, m + 1)
                    wait_pos(v, h_ready, m - 1)
                    for r in range(2):
                        s = slice(START[r], START[r] + SEQ[r])
                        nc.vector.tensor_scalar(hf[j % 2][:, s], nt[j % 2][:, s], gain[:, layer, which, j, r:r + 1],
                                                mod[:, layer, 24 * which + j, r:r + 1], ALU.mult, ALU.add).then_inc(n_hf, 1)

            def x_stage(layer, first, own, gate, after=None):
                def body(i):
                    for u in range(2):
                        n = first + 2 * i + u
                        v.wait_ge(job_done, n + 1)
                        for r in range(2):
                            o = xT[:, 2 * i + u, START[r]:START[r] + SEQ[r]]
                            ins = nc.vector.scalar_tensor_tensor(o, pj[u][:, P + START[r]:P + START[r] + SEQ[r]],
                                                                 mod[:, layer, gate + 2 * i + u, r:r + 1], o, ALU.mult, ALU.add)
                            ins.then_inc((up0, evac[u])[r], 1)
                        next_low(first, i, u, own)
                    if after is not None:
                        after(i)
                pairs(v, KD, body)

            def ffn(layer):
                vec = (vecB, vecC)[layer]
                for half in range(2):
                    first = J_UP[layer][half]
                    seen = (2 * layer + half) * FH

                    def body(i, first=first, seen=seen, half=half):
                        next_low(first, i, 0, KD)
                        f = half * FH + i
                        v.wait_ge(evac[0], first // 2 + i + 1)
                        n1 = TOK + 1
                        taps = [vec[:, 22 * w + f:22 * w + f + 1] for w in range(3)] if isinstance(f, int) else \
                               [vec[:, bass.ds(22 * w + f, 1)] for w in range(3)]
                        shift = vec[:, 66 + f:67 + f] if isinstance(f, int) else vec[:, bass.ds(66 + f, 1)]
                        nc.vector.tensor_scalar(conv[:, 0:n1], gpad[:, 1:1 + n1], taps[1], shift, ALU.mult, ALU.add).then_inc(cv, 1)
                        v.wait_ge(cv, 3 * (seen + i) + 1)
                        nc.vector.scalar_tensor_tensor(conv[:, 0:n1], gpad[:, 0:n1], taps[0], conv[:, 0:n1], ALU.mult, ALU.add).then_inc(cv, 1)
                        v.wait_ge(cv, 3 * (seen + i) + 2)
                        nc.vector.scalar_tensor_tensor(conv[:, 0:n1], gpad[:, 2:2 + n1], taps[2], conv[:, 0:n1], ALU.mult, ALU.add).then_inc(cv, 1)
                        next_low(first, i, 1, KD)
                        v.wait_ge(sl, seen + i + 1)
                        v.wait_ge(job_done, first + 2 * i + 2)
                        nc.vector.tensor_tensor(hidf[:, 0:SEQ[0]], conv[:, 0:SEQ[0]], pj[1][:, P:P + SEQ[0]], ALU.mult).then_inc(up0, 1)
                        nc.vector.tensor_tensor(hidf[:, SEQ[0]:TOK], conv[:, SEQ[0] + 1:TOK + 1], pj[1][:, P + SEQ[0]:P + TOK],
                                                ALU.mult).then_inc(evac[1], 1)
                        v.wait_ge(hh, seen + i + 1)
                        nc.vector.tensor_tensor(hid_lo[:, i, :], hidf[:, :], hid_hi[:, i, :].bitcast(F32), ALU.subtract).then_inc(hl, 1)
                        if layer == 0:
                            ada_step(1, (16, 29)[half] + i)
                    pairs(v, 2 * FH, body)

                    def after(i):
                        if isinstance(i, int):
                            ada_step(1, 27 if i == 0 else 28)
                    x_stage(layer, J_DOWN[layer][half], FH, 40, after if layer == 0 and half == 0 else None)

            norm(0)
            v.wait_ge(h_ready, KD)

            def in_body(i):
                for u in range(2):
                    n = 2 * i + u
                    ada_step(0, n)
                    next_low(0, i, u, KD)
                    if isinstance(n, int) and n == 2:
                        v.wait_ge(s5g, 1)
                        nc.vector.reciprocal(s5v[:, 13, :], s5v[:, 13, :]).then_inc(s5r, 1)
            in_body(0)
            in_body(1)
            with v.Fori(2, 7) as i:
                in_body(i)
            in_body(7)
            v.wait_ge(ada_tr, 16)
            modulation(0, 16, 48, pb[:, 32:96], 2)
            gains(0, 1)
            v.wait_ge(q_sd, 1)
            nc.vector.reciprocal(qrms[:, :, :], qrms[:, :, :]).then_inc(q_rc, 1)
            for k in range(8):
                v.wait_ge(q_bc, k + 1)
                g = vecB[:, QG + k // 4:QG + 1 + k // 4]
                nc.vector.scalar_tensor_tensor(z0[:, k, :], z0[:, k, :], g, pj[k % 2][:, wide], ALU.mult, ALU.mult).then_inc(q_ready, 1)
            v.wait_ge(q_ready, 8)
            v.wait_ge(s5g, 2)
            def inputs(q):
                wait_pos(v, rt_tr, 4 * q)
                ks = slice(4 * q, 4 * q + 4)
                pr, pi = (powr[r][:, 0, ks, 0:STEPS][:, :, ::-1].unsqueeze(3).broadcast_to([P, 4, STEPS, CH]) for r in range(2))
                br, bi = (bb[0][r][:, ks, :].unsqueeze(2).broadcast_to([P, 4, STEPS, CH]) for r in range(2))
                t1, t2 = (rtmp[0][i][:, :, :, :] for i in range(2))
                tt(t1, pr, br, ALU.mult)
                tt(t2, pi, bi, ALU.mult)
                tt(rs[0][0][:, :, :, :], t1, t2, ALU.subtract)
                tt(t1, pr, bi, ALU.mult)
                tt(t2, pi, br, ALU.mult)
                nc.vector.tensor_tensor(rs[0][1][:, :, :, :], t1, t2, ALU.add).then_inc(rs_f, 1)
                v.wait_ge(rs_f, q + 1)
            inputs(0)
            v.wait_ge(x_zero, 1)
            for q in range(4):
                if q < 3:
                    inputs(q + 1)
                for b in range(4):
                    k = 4 * q + b
                    v.wait_ge(r_mm, k + 1)
                    src = pn[:, 512 * (b % 2):512 * (b % 2) + 4 * NCH].rearrange("p (d r n) -> p d r n", d=2, r=2)
                    for d in range(2):
                        for r in range(2):
                            m, c0 = CHUNKS[r], START[r] // STEPS
                            part = src[:, d, :, c0:c0 + m]
                            if d:
                                part = part[:, :, ::-1]
                            ins = nc.vector.tensor_copy(xs[:, 1:1 + m, :, d, r, k].rearrange("p m r -> p r m"), part)
                            ins.then_inc(r_ev, 1)
            v.wait_ge(r_ev, 64)
            for b in range(6):
                v.wait_ge(v_tr, b + 1)
                nc.vector.tensor_copy(vn[:, b, :], bank[b % 4]).then_inc(v_ready, 1)

            def scores(n):
                h, qt = divmod(n, TT)
                w = SEQ[0] if qt < 2 else SEQ[1]
                q0 = qt if qt < 2 else qt - 2
                if qt == 0:
                    if h == 0:
                        v.wait_ge(mask_in, 32)
                    wait_pos(v, a_m, TT * (h - 1))
                    nc.vector.scalar_tensor_tensor(bias[h % 2][:, :], dist[:, :], -(2.0 ** -(8.0 * (h + 1) / HEADS)), lnc[:, :],
                                                   ALU.mult, ALU.add).then_inc(bias_ready, 1)
                    v.wait_ge(bias_ready, h + 1)
                v.wait_ge(a_s, n + 1)
                wait_pos(v, a_t, n - 2)
                nc.vector.tensor_tensor_reduce(att_s[n % 3][:, 0:w], pn[:, 512 * (n % 2):512 * (n % 2) + w],
                                               bias[h % 2][:, OVER - P * q0:OVER - P * q0 + w], 1.0, -3.0e38,
                                               ALU.add, ALU.max, att_m[:, n:n + 1]).then_inc(a_m, 1)
                v.wait_ge(a_m, n + 1)
                nc.vector.tensor_scalar(att_nm[:, n:n + 1], att_m[:, n:n + 1], -1.0, None, ALU.mult).then_inc(a_nm, 1)

            def weigh(n):
                h, qt = divmod(n, TT)
                v.wait_ge(a_p, n + 1)
                nc.vector.reciprocal(att_rl[:, n:n + 1], att_l[:, n:n + 1]).then_inc(a_rl, 1)
                v.wait_ge(a_rl, n + 1)
                v.wait_ge(a_o, n + 1)
                nc.vector.tensor_scalar(yb[:, qt, HD * h:HD * h + HD], bank[n % 2][:, 0:HD],
                                        att_rl[:, n:n + 1], None, ALU.mult).then_inc(a_y, 1)
            def output_step(q, step):
                if step == 0:
                    wait_pos(v, o_mm, 2 * (q - 2))
                d, part = divmod(step, 6)
                ks = slice(4 * q, 4 * q + 4)
                cr, ci, cn = (ct[r][:, ks, :].unsqueeze(2).broadcast_to([P, 4, STEPS + 1, CH]) for r in range(3))
                pr, pi = ((powr[r][:, 1, ks, ::-1] if d else powr[r][:, 0, ks, :]).unsqueeze(3).broadcast_to([P, 4, STEPS + 1, CH])
                          for r in range(2))
                t1, t2 = ctmp[0][:, :, :, :], ctmp[1][:, :, :, :]
                if part == 0:
                    tt(t1, pr, cr, ALU.mult)
                elif part == 1:
                    tt(t2, pi, ci, ALU.mult)
                elif part == 2:
                    tt(cp[q % 3][d][0][:, :, :, :], t1, t2, ALU.subtract)
                elif part == 3:
                    tt(t1, pi, cn, ALU.mult)
                elif part == 4:
                    tt(t2, pr, ci, ALU.mult)
                else:
                    nc.vector.tensor_tensor(cp[q % 3][d][1][:, :, :, :], t1, t2, ALU.subtract).then_inc((cp_f, cp_b)[d], 1)
                    v.wait_ge((cp_f, cp_b)[d], q + 1)
            scores(0)
            scores(1)
            for n in range(48):
                if n < 46:
                    scores(n + 2)
                if 8 <= n < 20:
                    output_step(0, n - 8)
                if n:
                    weigh(n - 1)
            weigh(47)

            v.wait_ge(a_s, 48)
            for q in (1, 2):
                for step in range(12):
                    output_step(q, step)
            for q in range(4):
                for b in range(2):
                    v.wait_ge(y_tr, 2 * q + b + 1)
                    src = (pa, pb)[b][:, 0:4 * NCH].rearrange("p (i n) -> p i n", i=4)
                    dst = ya[:, q, :].rearrange("p (n i) -> p i n", i=STEPS)[:, 4 * b:4 * b + 4, :]
                    nc.vector.tensor_copy(dst, src).then_inc(y_ev, 1)
                if q == 0:
                    for step in range(12):
                        output_step(3, step)
            for k in range(4):
                v.wait_ge(ya_h, k + 1)
                nc.vector.tensor_tensor(ya_lo[:, k, :], ya[:, k, :], ya_hi[:, k, :].bitcast(F32), ALU.subtract).then_inc(ya_l, 1)
                v.wait_ge(yb_hi, k + 1)
                nc.vector.tensor_tensor(mixb_lo[:, k, :], pj[k % 2][:, wide], mixb_hi[:, k, :].bitcast(F32), ALU.subtract).then_inc(yb_lo, 1)
            for k in range(4):
                u = k % 2
                next_low(J_GLU, k // 2, u, 4)
                v.wait_ge(evac[u], (J_GLU + k) // 2 + 1)
                nc.vector.tensor_tensor(sig[u][:, :], sig[u][:, :], ya[:, k, :], ALU.mult).then_inc(glu_m, 1)
                v.wait_ge(glu_h, k + 1)
                nc.vector.tensor_tensor(mixa_lo[:, k, :], sig[u][:, :], mixa_hi[:, k, :].bitcast(F32), ALU.subtract).then_inc(glu_l, 1)
            x_stage(0, J_OUT[0], KD, 16)
            norm(1)
            ffn(0)
            v.wait_ge(ada_tr, 40)
            modulation(1, 0, 48, pb[:, 0:96], 3)
            for which in range(2):
                gains(1, which)
            norm(2)

            def plain(first, cnt, own):
                def body(i):
                    for u in range(2):
                        next_low(first, i, u, own)
                pairs(v, cnt, body)
            plain(J_IN[1], 12, KD)
            v.wait_ge(evac[0], J_IN[1] // 2 + 6)
            v.wait_ge(evac[1], J_IN[1] // 2 + 6)
            v.wait_ge(pad_zero, 6)
            n1 = TOK + 1
            seq = [0]

            def chain(ins):
                seq[0] += 1
                ins.then_inc(d_seq, 1)
                v.wait_ge(d_seq, seq[0])
            for k in range(4):
                gc, hs, gb = z1[:, 8 + k, :], z1[:, k, :], z1[:, 4 + k, :]
                taps = [vecB[:, 92 + 4 * w + k:93 + 4 * w + k] for w in range(3)]
                chain(nc.vector.tensor_tensor(prod[:, 1:1 + SEQ[0]], gc[:, 0:SEQ[0]], hs[:, 0:SEQ[0]], ALU.mult))
                chain(nc.vector.tensor_tensor(prod[:, 2 + SEQ[0]:2 + TOK], gc[:, SEQ[0]:TOK], hs[:, SEQ[0]:TOK], ALU.mult))
                chain(nc.vector.tensor_scalar(pconv[:, 0:n1], prod[:, 1:1 + n1], taps[1], None, ALU.mult))
                chain(nc.vector.scalar_tensor_tensor(pconv[:, 0:n1], prod[:, 0:n1], taps[0], pconv[:, 0:n1], ALU.mult, ALU.add))
                chain(nc.vector.scalar_tensor_tensor(pconv[:, 0:n1], prod[:, 2:2 + n1], taps[2], pconv[:, 0:n1], ALU.mult, ALU.add))
                chain(nc.vector.tensor_tensor(yd[:, 0:SEQ[0]], pconv[:, 0:SEQ[0]], gb[:, 0:SEQ[0]], ALU.mult))
                nc.vector.tensor_tensor(yd[:, SEQ[0]:TOK], pconv[:, SEQ[0] + 1:n1], gb[:, SEQ[0]:TOK], ALU.mult).then_inc(d_f, 1)
                next_low(J_IN[1] + 12, k // 2, k % 2, KD)
                v.wait_ge(d_h, k + 1)
                nc.vector.tensor_tensor(mixd_lo[:, k, :], yd[:, :], mixd_hi[:, k, :].bitcast(F32), ALU.subtract).then_inc(d_l, 1)
            for k in range(4):
                v.wait_ge(fy_hi, k + 1)
                nc.vector.tensor_tensor(mixc_lo[:, k, :], pj[k % 2][:, wide], mixc_hi[:, k, :].bitcast(F32), ALU.subtract).then_inc(fy_lo, 1)
            x_stage(1, J_OUT[1], KD, 16)
            norm(3)
            ffn(1)
            for n in range(2 * TT):
                v.wait_ge(out_tr, n + 1)
                nc.vector.tensor_copy(orow[n // 2][:, 512 * (n % 2):512 * (n % 2) + 512], bank[n % 4]).then_inc(out_ev, 1)

        @block.tensor
        def _(pe):
            mm = nc.tensor.matmul

            def job(n, u, k, rhs_hi, rhs_lo, ready=None):
                pe.wait_ge(w_lo_ready, n + 1)
                for j in range(k):
                    if ready is not None:
                        pe.wait_ge(ready[0], ready[1] + j + 1)
                    for p, (w, x) in enumerate(((w_hi, rhs_hi), (w_hi, rhs_lo), (w_lo, rhs_hi))):
                        for c in range(2):
                            ins = mm(pj[u][:, P + c * HALF:P + (c + 1) * HALF], w[u][:, j, :], x(j)[:, c * HALF:(c + 1) * HALF],
                                     start=(j == 0 and p == 0), stop=(j == k - 1 and p == 2))
                ins.then_inc(job_done, 1)

            def jobs(first, cnt, k, rhs_hi, rhs_lo, ready=None, after=None, peel=1):
                def body(i):
                    for u in range(2):
                        wait_pos(pe, evac[u], first // 2 + i)
                        job(first + 2 * i + u, u, k, rhs_hi, rhs_lo, ready if isinstance(i, int) and i == 0 and u == 0 else None)
                        if after is not None:
                            after(i, u)
                pairs(pe, cnt, body, peel)

            def ada_sum(layer, e):
                pe.wait_ge(ada_v, 16 * (e + 1))
                wait_pos(pe, ada_row_ready, e)
                for r in range(2):
                    ins = mm(pa[0:2, 0:ADA], pick[:, r, :], ada_acc[layer][r] if layer else ada_acc0[r][:, :],
                             start=(r == 0), stop=(r == 1))
                ins.then_inc(ada_red, 1)

            def ada_spread(layer, e):
                pe.wait_ge(ada_row_ready, e + 1)
                for s in range(ADA // P):
                    c = 32 + 4 * e + 2 * s if layer == 0 else 4 * (e - 16) + 2 * s
                    o = pb[:, c:c + 2] if isinstance(c, int) else pb[:, bass.ds(c, 2)]
                    ins = mm(o, ada_row[layer][0:2, P * s:P * s + P], ident[0:2, 0:2], start=True, stop=True)
                ins.then_inc(ada_tr, 1)

            def tile_sum(j, sq):
                pe.wait_ge(n_sq, j + 1)
                for b in range(TT):
                    ins = mm(pn[:, b:b + 1], sq[:, P * b:P * b + P], ones[:, 0:1], start=(j == 0 and b == 0),
                             stop=(j == KD - 1), skip_group_check=True)
                ins.then_inc(n_mm, 1)

            def norm(k):
                if k:
                    pe.wait_ge(n_add, KD * k)
                    for b in range(TT):
                        ins = mm(pn[:, b:b + 1], sq_acc[:, P * b:P * b + P], ones[:, 0:1], start=True, stop=True)
                    ins.then_inc(n_mm, 1)
                pe.wait_ge(n_rs, k + 1)
                for b in range(TT):
                    ins = mm(pn[:, P + P * b:2 * P + P * b], rms[:, b:b + 1].broadcast_to([P, P]), ident[:, :], start=True, stop=True)
                ins.then_inc(n_bc, 1)

            pe.wait_ge(const_in, 32)
            pe.wait_ge(c_in, 32)
            nc.tensor.transpose(pa[:, 0:2 * KD], crows[:, :], ident[0:2 * KD, 0:2 * KD]).then_inc(c_tr, 1)
            pe.wait_ge(x_in, 32)
            for n in range(12):
                wait_pos(pe, xt_ev, n - 3)
                for k in range(4):
                    ins = nc.tensor.transpose(bank[n % 4][:, P * k:P * k + P],
                                              xrows[:, n // 2, P * (4 * (n % 2) + k):P * (4 * (n % 2) + k) + P], ident[:, :])
                ins.then_inc(xt_ps, 1)

            def vectors():
                pe.wait_ge(rows_in, 16 * ROW_DMAS)
                pe.wait_ge(expanded, 1)
                for k, (rows, n) in enumerate(((rowsA, P), (rowsB, QG + 2), (rowsC, 88), (rowsS, 96))):
                    nc.tensor.transpose(bank[1][:, P * k:P * k + n], rows[0:n, :], ident[0:n, 0:n]).then_inc(vec_ps, 1)
                pe.wait_ge(s5_in, 16 * 9)
                for r in range(2):
                    for k in range(4):
                        ins = nc.tensor.transpose(bank[2 + r][:, P * k:P * k + P], crow[r][:, k, :, :].rearrange("p h s -> p (h s)"), ident[:, :])
                    ins.then_inc(c_ps, 1)

            def spread_row(k):
                pe.wait_ge(row_ev, k + 1)
                for s in range(4):
                    c = 2 * (4 * k + s)
                    ins = mm(bank[0][:, c:c + 2], mod_row[k % 2][:, P * s:P * s + P], ident[0:2, 0:2], start=True, stop=True)
                ins.then_inc(row_tr, 1)
            pe.wait_ge(cond_ready, 1)
            pe.wait_ge(fill, 4)
            pe.wait_ge(xt_ev, 12)
            for k in range(4):
                pe.wait_ge(ada_a_in[k % 3], 16 * (k // 3 + 1))
                wait_pos(pe, row_ev, k - 1)
                for j in range(KD):
                    ins = mm((pa, pb)[k % 2][0:2, :], cond[:, j, :], ada_a[k % 3][:, j, :], start=(j == 0), stop=(j == KD - 1))
                ins.then_inc(rows_done, 1)
                if k:
                    spread_row(k - 1)
                for j in (2 * k, 2 * k + 1):
                    tile_sum(j, sq_first[j % 2])
                if k == 1:
                    vectors()
            spread_row(3)
            norm(0)

            def h_parts(j):
                return h_hi[:, j, :]

            def l_parts(j):
                return h_lo[:, j, :]

            def in_body(i):
                for u in range(2):
                    n = 2 * i + u
                    fixed = isinstance(n, int)
                    wait_pos(pe, evac[u], i)
                    if fixed and n == 0:
                        pe.wait_ge(mod_ready, 1)
                    if fixed and n == 1:
                        pe.wait_ge(vec_ev, 5)
                    job(n, u, KD, h_parts, l_parts, (h_ready, 0) if fixed and n == 0 else None)
                    if fixed and 1 <= n <= 4:
                        pe.wait_ge(evac[(n - 1) % 2], (n - 1) // 2 + 1)
                        wait_pos(pe, ut_ev, 2 * (n - 1))
                        for j in range(STEPS):
                            ins = nc.tensor.transpose(pn[0:NCH, P * j:P * j + P], ut[(n - 1) % 2][:, j:TOK:STEPS], ident[:, :])
                        ins.then_inc(ut_tr, 1)
                    if not (fixed and n < 1):
                        ada_spread(0, n - 1)
                    ada_sum(0, n)
            for i in range(3):
                in_body(i)
            with pe.Fori(3, 7) as i:
                in_body(i)
            in_body(7)
            ada_spread(0, 15)
            pe.wait_ge(ut_ev, 8)
            for k in range(8):
                pe.wait_ge(q_sq, k + 1)
                for b in range(TT):
                    c = 2 * HEADS * b + 2 * k
                    ins = mm(pn[:, c:c + 2], qsq[k % 2][:, P * b:P * b + P], blk[:, :], start=True, stop=True)
                ins.then_inc(q_mm, 1)
            pe.wait_ge(q_rc, 1)
            for u in range(2):
                pe.wait_ge(evac[u], 8)
            for b in range(TT):
                ins = nc.tensor.transpose(pj[0][0:2 * HEADS, P + P * b:2 * P + P * b], qrms[:, b, :], ident[:, :])
            ins.then_inc(q_rt, 1)
            pe.wait_ge(q_re, 1)
            pe.wait_ge(spread_in, 16)
            for k in range(8):
                wait_pos(pe, q_ready, k - 1)
                for c in range(2):
                    ins = mm(pj[k % 2][:, P + c * HALF:P + (c + 1) * HALF], spread[:, k, :], q_rows[:, c * HALF:(c + 1) * HALF],
                             start=True, stop=True)
                ins.then_inc(q_bc, 1)
            pe.wait_ge(q_ready, 8)
            def chunks(q):
                for b in range(2):
                    wait_pos(pe, u_ev, 2 * q - 1 + b)
                    for g in range(4):
                        ins = nc.tensor.transpose((pa, pb)[b][:, NCH * g:NCH * g + NCH],
                                                  un[:, 8 * q + 4 * b + g, :, :].rearrange("n j c -> n (j c)"), ident[0:NCH, 0:NCH])
                    ins.then_inc(u_tr, 1)
            chunks(0)
            for q in range(4):
                pe.wait_ge(rs_f, q + 1)
                pe.wait_ge(rs_b, q + 1)
                for b in range(4):
                    for k in range(4):
                        ins = nc.tensor.transpose(bank[b][:, P * k:P * k + P],
                                                  rs[b // 2][b % 2][:, k, :, :].rearrange("p j c -> p (j c)"), ident[:, :])
                    ins.then_inc(rt_tr, 1)
                if q < 3:
                    chunks(q + 1)
                pe.wait_ge(u_ev, 2 * q + 2)
                pe.wait_ge(rt_ev, 4 * q + 4)
                for k in range(4):
                    wait_pos(pe, r_ev, 4 * (4 * q + k - 1))
                    for d in range(4):
                        for h in range(2):
                            ins = mm(pn[64 * h:64 * h + 64, 512 * (k % 2) + NCH * d:512 * (k % 2) + NCH * (d + 1)],
                                     rt[:, k, h, d // 2, d % 2, :], uc[:, 8 * q + 2 * k + h, :], start=True, stop=True)
                    ins.then_inc(r_mm, 1)
            for b in range(6):
                wait_pos(pe, v_ready, b - 3)
                for k in range(4):
                    ins = nc.tensor.transpose(bank[b % 4][:, P * k:P * k + P], z0[:, 8 + k, P * b:P * b + P], ident[:, :])
                ins.then_inc(v_tr, 1)
            pe.wait_ge(r_ev, 64)
            pe.wait_ge(v_ready, 6)

            def geo(n):
                h, qt = divmod(n, TT)
                r = 0 if qt < 2 else 1
                return h, qt, START[r], SEQ[r]

            def score(n):
                h, qt, k0, w = geo(n)
                wait_pos(pe, a_m, n - 1)
                rows = slice(HD * (h % 2), HD * (h % 2) + HD)
                mm(pn[:, 512 * (n % 2):512 * (n % 2) + w], z0[rows, h // 2, P * qt:P * qt + P], z0[rows, 4 + h // 2, k0:k0 + w],
                   start=True, stop=True).then_inc(a_s, 1)

            def values(n):
                h, qt, k0, w = geo(n)
                pe.wait_ge(a_pt, n + 1)
                wait_pos(pe, a_y, n - 1)
                for k in range(w // P):
                    ins = mm(bank[n % 2][:, 0:HD], att_t[n % 2][:, k, :], vn[:, k0 // P + k, HD * h:HD * h + HD],
                             start=(k == 0), stop=(k == w // P - 1))
                ins.then_inc(a_o, 1)
            score(0)
            score(1)
            for n in range(48):
                if n < 46:
                    score(n + 2)
                h, qt, k0, w = geo(n)
                pe.wait_ge(a_p, n + 1)
                wait_pos(pe, a_pt, n - 1)
                for k in range(w // P):
                    ins = nc.tensor.transpose((pa, pb)[n % 2][:, P * k:P * k + P], att_s[n % 3][:, P * k:P * k + P], ident[:, :])
                ins.then_inc(a_t, 1)
                if n:
                    values(n - 1)
            values(47)
            pe.wait_ge(a_y, 48)
            pe.wait_ge(a_m, 48)

            def kernels(q):
                pe.wait_ge(cp_f, q + 1)
                pe.wait_ge(cp_b, q + 1)
                for b in range(2):
                    wait_pos(pe, k_ev, 4 * q)
                    wait_pos(pe, y_ev, 2 * (q - 1))
                    for k in range(2 * b, 2 * b + 2):
                        for h in range(2):
                            rows = slice(64 * h, 64 * h + 64)
                            o = kbank[b][h][0:CH, 256 * (k % 2):256 * (k % 2) + 256]
                            for d, c0, j0 in ((1, 0, 1), (0, 7 * CH, 0)):
                                for r in range(2):
                                    mm(o[:, c0:c0 + P], bb[d][r][rows, 4 * q + k, :],
                                       cp[q % 3][d][r][rows, k, j0:j0 + STEPS, :].rearrange("p j c -> p (j c)"),
                                       start=(d == 1 and r == 0), stop=False, skip_group_check=True)
                            ins = mm(o[:, 7 * CH:8 * CH], ident[0:CH, 0:CH], ddiag[:, 8 * q + 2 * k + h, :],
                                     start=False, stop=True, skip_group_check=True)
                    ins.then_inc(k_mm, 1)
            kernels(0)
            for q in range(4):
                if q < 3:
                    kernels(q + 1)
                pe.wait_ge(sp_ready, 8 * q + 8)
                pe.wait_ge(t_in, 128 * (q + 1))
                for b in range(2):
                    wait_pos(pe, o_ev, 2 * q)
                    for k in range(4):
                        rows = slice(64 * b, 64 * b + 64)
                        o = bank[b][0:NCH, P * k:P * k + P]
                        mm(o, uc[:, 8 * q + 2 * k + b, :], tm[q % 2][:, 2 * k + b, :], start=True, stop=False)
                        for d in range(2):
                            for r in range(2):
                                ins = mm(o, sp[q % 2][rows, d, r, k, :],
                                         cp[q % 3][d][r][rows, k, 1 - d:1 - d + STEPS, :].rearrange("p j c -> p (j c)"),
                                         start=False, stop=(d == 1 and r == 1))
                    ins.then_inc(o_mm, 1)
                pe.wait_ge(o_ev, 2 * q + 2)
                pe.wait_ge(k_ev, min(4 * q + 8, 16))
                for b in range(2):
                    wait_pos(pe, y_ev, 2 * q)
                    for i in range(4):
                        ins = nc.tensor.transpose((pa, pb)[b][:, NCH * i:NCH * i + NCH], yn[:, 4 * b + i, :], ident[0:NCH, 0:NCH])
                    ins.then_inc(y_tr, 1)
            for k in range(4):
                wait_pos(pe, yb_lo, k - 1)
                for b in range(TT):
                    ins = nc.tensor.transpose(pj[k % 2][:, P + P * b:P + P * b + P], yb[:, b, P * k:P * k + P], ident[:, :])
                ins.then_inc(yb_tr, 1)
            pe.wait_ge(yb_lo, 4)
            jobs(J_GLU, 4, 4, lambda j: ya_hi[:, j, :], lambda j: ya_lo[:, j, :], (ya_l, 0))
            pe.wait_ge(glu_l, 4)
            jobs(J_OUT[0], KD, KD, lambda j: (mixa_hi if j < 4 else mixb_hi)[:, j % 4, :],
                 lambda j: (mixa_lo if j < 4 else mixb_lo)[:, j % 4, :])

            def ffn(layer):
                norm(2 * layer + 1)
                for half in range(2):
                    def after_up(i, u, half=half):
                        if half == 0 and isinstance(i, int) and i <= 1 - u:
                            return
                        if u == 0:
                            ada_spread(1, (14, 27)[half] + i)
                        else:
                            ada_sum(1, (15, 28)[half] + i)

                    def after_down(i, u, half=half):
                        if half == 0 and isinstance(i, int):
                            (ada_spread, ada_sum)[u](1, (25 if i == 0 else 26) + u)
                        if half == 1 and isinstance(i, int) and i == 0:
                            (ada_spread, ada_sum)[u](1, 38 + u)
                        if half == 1 and isinstance(i, int) and i > 0 and u == 0:
                            ada_spread(1, 39)
                    jobs(J_UP[layer][half], 2 * FH, KD, h_parts, l_parts, (h_ready, KD * (2 * layer + 1)) if half == 0 else None,
                         after_up if layer == 0 else None, 2 if layer == 0 and half == 0 else 1)
                    jobs(J_DOWN[layer][half], KD, FH, lambda j: hid_hi[:, j, :], lambda j: hid_lo[:, j, :],
                         (hl, FH * (2 * layer + half)), after_down if layer == 0 else None)
            ffn(0)
            norm(2)
            jobs(J_IN[1], 12, KD, h_parts, l_parts, (h_ready, 2 * KD))
            jobs(J_IN[1] + 12, 4, KD, h_parts, l_parts)
            pe.wait_ge(cs_in, 16)
            for u in range(2):
                pe.wait_ge(evac[u], J_OUT[1] // 2)
            for n in range(2 * TT):
                wait_pos(pe, f_ev, n - 3)
                for s in range(2):
                    ins = mm(bank[n % 4][:, 256 * s:256 * s + 256], z1[:, 12 + 2 * (n % 2) + s, P * (n // 2):P * (n // 2) + P], cs[:, :],
                             start=True, stop=True)
                ins.then_inc(f_mm, 1)
            pe.wait_ge(f_ev, 2 * TT)
            pe.wait_ge(dft_in, 16 * 4)
            for k in range(4):
                wait_pos(pe, fy_lo, k - 1)
                u = k % 2
                for s in range(2):
                    for b in range(2):
                        mm(pj[u][:, P:P + SEQ[0]], fv[:, b, k, P * s:P * s + P], dftp[:, s, b, :],
                           start=(s == 0 and b == 0), stop=(s == 1 and b == 1))
                for c0, c1 in ((0, 128), (128, 512)):
                    for s in range(2):
                        for b in range(4):
                            ins = mm(pj[u][:, P + SEQ[0] + c0:P + SEQ[0] + c1], fv[:, 2 + b, k, P * s:P * s + P], dft[:, s, b, c0:c1],
                                     start=(s == 0 and b == 0), stop=(s == 1 and b == 3))
                ins.then_inc(fy_mm, 1)
            pe.wait_ge(d_l, 4)
            pe.wait_ge(fy_lo, 4)
            jobs(J_OUT[1], KD, KD, lambda j: (mixc_hi if j < 4 else mixd_hi)[:, j % 4, :],
                 lambda j: (mixc_lo if j < 4 else mixd_lo)[:, j % 4, :])
            ffn(1)
            for u in range(2):
                pe.wait_ge(evac[u], JOBS // 2)
            for n in range(2 * TT):
                wait_pos(pe, out_ev, n - 3)
                for k in range(4):
                    ins = nc.tensor.transpose(bank[n % 4][:, P * k:P * k + P], xT[:, 4 * (n % 2) + k, P * (n // 2):P * (n // 2) + P],
                                              ident[:, :])
                ins.then_inc(out_tr, 1)


INS = ["x_prompt", "x_sample", "c_prompt", "c_sample", "ada_w", "ada_b", "norm_mix_g", "norm_ffn_g", "ffn_w_gate",
       "ffn_w_up", "ffn_conv_w", "ffn_conv_b", "ffn_w_down", "ab_w_in", "ab_w_out", "s5_lam_re_f", "s5_lam_im_f",
       "s5_log_dt_f", "s5_lam_re_b", "s5_lam_im_b", "s5_log_dt_b", "s5_b_re", "s5_b_im", "s5_c_re", "s5_c_im", "s5_d",
       "s5_w_glu", "s5_b_glu", "q_norm_g", "k_norm_g", "cd_w_in", "cd_w_out", "sconv_w"]


def constants():
    head = np.kron(np.eye(P // HD), np.ones((HD, HD)))
    d = np.arange(P)[:, None] - (np.arange(OVER + 512)[None, :] - OVER)
    dist = np.abs(d)
    branches = sum(((dist % dil == 0) & (dist <= win // 2)).astype(np.int64) for win, dil in ((128, 1), (512, 4), (2048, 16)))
    lnc = np.where(branches > 0, np.log(np.maximum(branches, 1)), -1e30)

    def fourier(n):
        a = 2 * np.pi * (np.outer(np.arange(n), np.arange(n)) % n) / n
        return np.cos(a) / math.sqrt(n), np.sin(a) / math.sqrt(n)
    c, s = fourier(P)
    spread = (np.arange(2 * HEADS)[:, None, None] == 2 * np.arange(8)[None, :, None] + (np.arange(P) // HD)[None, None, :])
    big, small = fourier(SEQ[1]), fourier(SEQ[0])
    out = {"c_ident": np.eye(P), "c_blk": head[:, ::HD], "c_dist": dist, "c_lnc": lnc, "c_cs": np.concatenate([c, s], 1), "c_spread": spread,
           "c_dft": np.stack([big[0], -big[1]]), "c_dftp": np.stack([small[0], -small[1]])}
    return {k: np.ascontiguousarray(v, dtype=np.float32) for k, v in out.items()}


def kernel(**inputs):
    import concourse.bacc as bacc
    from concourse.bass_utils import run_bass_kernel_spmd

    nc = bacc.Bacc("TRN2", target_bir_lowering=False, num_devices=1)
    arrays, tensors = {}, {}
    for name, a in [(n, inputs[n]) for n in INS] + list(constants().items()):
        a = np.ascontiguousarray(a)
        arrays["in_" + name] = a
        tensors[name] = nc.dram_tensor("in_" + name, a.shape, mybir.dt.from_np(a.dtype), kind="ExternalInput").ap()
    outs = [nc.dram_tensor(n, (1, s, D), F32, kind="ExternalOutput").ap() for n, s in (("y_prompt", SEQ[0]), ("y_sample", SEQ[1]))]
    build(nc, tensors, *outs)
    r = run_bass_kernel_spmd(nc, [arrays], core_ids=[0])
    return r.results[0]["y_prompt"], r.results[0]["y_sample"]
```
